# Optimizing a Trainium2 kernel written in Bass

```python
import math
import jax, jax.numpy as jnp
from jax import lax
import numpy as np

D_MODEL = 1024
BATCH = 1
SEQ = 1024
DEPTH = 1

SB_HEAD_DIM = 64
SB_WIDTH = D_MODEL // 4
SB_HEADS = SB_WIDTH // SB_HEAD_DIM
SB_BLOCK = 128
DN_HEAD_DIM = 128
DN_WIDTH = D_MODEL // 2
DN_HEADS = DN_WIDTH // DN_HEAD_DIM
DN_CONV = 4
DN_CHUNK = 64
HG_VAL_DIM = 64
HG_KEY_DIM = 64
HG_WIDTH = D_MODEL // 4
HG_HEADS = HG_WIDTH // HG_VAL_DIM
HG_KEY_WIDTH = HG_HEADS * HG_KEY_DIM
HG_CHUNK = 16
D_MIX = SB_WIDTH + DN_WIDTH + HG_WIDTH
SPLIT_SIZES = (SB_WIDTH, SB_WIDTH, SB_WIDTH,
               3 * DN_WIDTH, DN_WIDTH, DN_HEADS, DN_HEADS,
               HG_KEY_WIDTH, HG_KEY_WIDTH, HG_WIDTH, HG_WIDTH)
D_IN_PROJ = sum(SPLIT_SIZES)
D_FF = -(-8 * D_MODEL // (3 * 256)) * 256
EPS = 1e-6

kernel_name = "hybrid_sb_gdn_hgrn2_trunk"

def rms_norm(x, gain):
    xf = x.astype(jnp.float32)
    y = xf * lax.rsqrt(jnp.mean(xf * xf, axis=-1, keepdims=True) + EPS)
    return (y * gain.astype(jnp.float32)).astype(x.dtype)

def l2_norm(x):
    xf = x.astype(jnp.float32)
    return xf * lax.rsqrt(jnp.sum(xf * xf, axis=-1, keepdims=True) + EPS)

def split_heads(x, n_heads):
    b, s, _ = x.shape
    return x.reshape(b, s, n_heads, -1)

def causal_depthwise_conv(x, w):
    k_size, ch = w.shape
    return lax.conv_general_dilated(
        x, w[:, None, :].astype(x.dtype), window_strides=(1,),
        padding=[(k_size - 1, 0)], dimension_numbers=("NWC", "WIO", "NWC"),
        feature_group_count=ch)

def stick_breaking_attention(q, k, v):
    b, s, h, d = q.shape
    nb = s // SB_BLOCK
    scale = d ** -0.5
    qf = q.astype(jnp.float32)
    kf = k.astype(jnp.float32)
    vf = v.astype(jnp.float32)
    ar = jnp.arange(SB_BLOCK)
    rev_incl = (ar[:, None] >= ar[None, :]).astype(jnp.float32)
    outs = []
    for i in range(nb):
        n_keys = (i + 1) * SB_BLOCK
        q_i = qf[:, i * SB_BLOCK:(i + 1) * SB_BLOCK]
        k_p = kf[:, :n_keys]
        v_p = vf[:, :n_keys]
        z = jnp.einsum("bqhd,bkhd->bhqk", q_i, k_p) * scale
        past = jnp.arange(n_keys)[None, :] < (i * SB_BLOCK + ar)[:, None]
        log_keep = jnp.where(past, jax.nn.log_sigmoid(-z), 0.0)
        within = jnp.einsum("bhqnk,kj->bhqnj",
                            log_keep.reshape(b, h, SB_BLOCK, i + 1, SB_BLOCK), rev_incl)
        nblk = jnp.arange(i + 1)
        rev_excl = (nblk[:, None] > nblk[None, :]).astype(jnp.float32)
        offset = jnp.einsum("bhqn,nm->bhqm", within[..., 0], rev_excl)
        suffix = (within + offset[..., None]).reshape(b, h, SB_BLOCK, n_keys)
        w = jnp.exp(jnp.where(past, z + suffix, -jnp.inf))
        outs.append(jnp.einsum("bhqk,bkhd->bqhd", w, v_p))
    return jnp.concatenate(outs, axis=1).astype(q.dtype)

def _chunkify(x, c):
    b, s = x.shape[:2]
    return x.reshape(b, s // c, c, *x.shape[2:]).swapaxes(2, 3)

def gated_delta_rule(q, k, v, g, beta):
    b, s, h, dk = q.shape
    dv = v.shape[-1]
    c = DN_CHUNK
    q = _chunkify(q.astype(jnp.float32) * dk ** -0.5, c)
    k = _chunkify(k.astype(jnp.float32), c)
    v = _chunkify(v.astype(jnp.float32), c)
    g = _chunkify(g.astype(jnp.float32), c)
    beta = _chunkify(beta.astype(jnp.float32), c)
    causal = jnp.tril(jnp.ones((c, c), dtype=bool))
    strict = jnp.tril(jnp.ones((c, c), dtype=bool), k=-1)
    gc = jnp.einsum("bnhj,ij->bnhi", g, causal.astype(jnp.float32))
    diff = gc[..., :, None] - gc[..., None, :]
    decay = jnp.where(causal, jnp.exp(jnp.where(causal, diff, 0.0)), 0.0)
    k_beta = k * beta[..., None]
    v_beta = v * beta[..., None]
    m = jnp.where(strict, jnp.einsum("bnhid,bnhjd->bnhij", k_beta, k) * decay, 0.0)
    rhs = jnp.concatenate([v_beta, k_beta * jnp.exp(gc)[..., None]], axis=-1)
    sol = lax.linalg.triangular_solve(m, rhs, left_side=True, lower=True, unit_diagonal=True)
    u, w = sol[..., :dv], sol[..., dv:]
    attn_intra = jnp.einsum("bnhid,bnhjd->bnhij", q, k) * decay
    q_dec = q * jnp.exp(gc)[..., None]
    k_dec = k * jnp.exp(gc[..., -1:] - gc)[..., None]
    chunk_decay = jnp.exp(gc[..., -1])

    def step(state, xs):
        a_i, q_i, k_i, u_i, w_i, cd_i = xs
        v_new = u_i - jnp.einsum("bhck,bhkv->bhcv", w_i, state)
        o = jnp.einsum("bhck,bhkv->bhcv", q_i, state) + jnp.einsum("bhij,bhjv->bhiv", a_i, v_new)
        state = state * cd_i[..., None, None] + jnp.einsum("bhck,bhcv->bhkv", k_i, v_new)
        return state, o

    xs = tuple(jnp.moveaxis(t, 1, 0) for t in (attn_intra, q_dec, k_dec, u, w, chunk_decay))
    s0 = jnp.zeros((b, h, dk, dv), jnp.float32)
    _, o = lax.scan(step, s0, xs)
    return o.transpose(1, 0, 3, 2, 4).reshape(b, s, h, dv)

def hgrn2_recurrence(q, k, v, log_f):
    b, s, h, dk = q.shape
    dv = v.shape[-1]
    c = HG_CHUNK
    causal2 = jnp.tril(jnp.ones((c, c), dtype=bool))
    causal = causal2[..., None]
    tri = causal2.astype(jnp.float32)
    xs = tuple(jnp.moveaxis(_chunkify(t.astype(jnp.float32), c), 1, 0) for t in (q, k, v, log_f))

    def step(state, xs_i):
        q_i, k_i, v_i, lf_i = xs_i
        bcum = jnp.einsum("bhsk,ts->bhtk", lf_i, tri)
        o_inter = jnp.einsum("bhck,bhkv->bhcv", q_i * jnp.exp(bcum), state)
        diff = bcum[:, :, :, None, :] - bcum[:, :, None, :, :]
        dec = jnp.where(causal, jnp.exp(jnp.where(causal, diff, 0.0)), 0.0)
        scores = jnp.einsum("bhtsk,bhsk->bhts", dec * q_i[:, :, :, None, :], k_i)
        o = o_inter + jnp.einsum("bhts,bhsv->bhtv", scores, v_i)
        last = bcum[:, :, -1:, :]
        state = jnp.exp(last[:, :, 0, :])[..., None] * state + jnp.einsum(
            "bhsk,bhsv->bhkv", k_i * jnp.exp(last - bcum), v_i)
        return state, o

    s0 = jnp.zeros((b, h, dk, dv), jnp.float32)
    _, o = lax.scan(step, s0, xs)
    return o.transpose(1, 0, 3, 2, 4).reshape(b, s, h, dv)

def hybrid_layer(x, norm1, w_in, sb_gain, dn_conv, dn_a_log, dn_dt_bias, dn_gain,
                 hg_lb, hg_gain, w_out, norm2, w_gate, w_up, w_down):
    b, s, _ = x.shape
    h = rms_norm(x, norm1)
    proj = h @ w_in.astype(h.dtype)
    idx, acc = [], 0
    for n in SPLIT_SIZES[:-1]:
        acc += n
        idx.append(acc)
    (sb_q, sb_k, sb_v, dn_qkv, dn_z, dn_a, dn_b,
     hg_q, hg_f, hg_i, hg_g) = jnp.split(proj, idx, axis=-1)

    sb_o = stick_breaking_attention(split_heads(sb_q, SB_HEADS), split_heads(sb_k, SB_HEADS),
                                    split_heads(sb_v, SB_HEADS))
    sb_o = rms_norm(sb_o, sb_gain)

    dn_qkv = jax.nn.silu(causal_depthwise_conv(dn_qkv, dn_conv))
    dn_q, dn_k, dn_v = jnp.split(dn_qkv, 3, axis=-1)
    dn_g = -jnp.exp(dn_a_log.astype(jnp.float32)) * jax.nn.softplus(
        dn_a.astype(jnp.float32) + dn_dt_bias.astype(jnp.float32))
    dn_beta = jax.nn.sigmoid(dn_b.astype(jnp.float32))
    dn_o = gated_delta_rule(l2_norm(split_heads(dn_q, DN_HEADS)), l2_norm(split_heads(dn_k, DN_HEADS)),
                            split_heads(dn_v, DN_HEADS), dn_g, dn_beta).astype(x.dtype)
    dn_o = rms_norm(dn_o, dn_gain) * jax.nn.silu(split_heads(dn_z, DN_HEADS))

    lb = hg_lb.astype(jnp.float32)
    hf = hg_f.astype(jnp.float32)
    log_f = jnp.logaddexp(jnp.log(lb), jnp.log1p(-lb) + jax.nn.log_sigmoid(hf))
    hg_k = (1.0 - lb) * jax.nn.sigmoid(-hf)
    hg_o = hgrn2_recurrence(split_heads(jax.nn.silu(hg_q), HG_HEADS), split_heads(hg_k, HG_HEADS),
                            split_heads(hg_i, HG_HEADS), split_heads(log_f, HG_HEADS)).astype(x.dtype)
    hg_o = rms_norm(hg_o, hg_gain) * jax.nn.sigmoid(split_heads(hg_g, HG_HEADS))

    mix = jnp.concatenate([sb_o.reshape(b, s, SB_WIDTH), dn_o.reshape(b, s, DN_WIDTH),
                           hg_o.reshape(b, s, HG_WIDTH)], axis=-1)
    x = x + mix @ w_out.astype(mix.dtype)

    h2 = rms_norm(x, norm2)
    ff = jax.nn.silu(h2 @ w_gate.astype(h2.dtype)) * (h2 @ w_up.astype(h2.dtype))
    return x + ff @ w_down.astype(ff.dtype)

def setup_inputs(seed: int = 0) -> dict:
    key = jax.random.key(seed)
    ks = jax.random.split(key, 20)
    f32 = jnp.float32

    def gain(k, shape):
        return 1.0 + 0.02 * jax.random.normal(k, shape, f32)

    dt = jnp.exp(jax.random.uniform(ks[6], (DEPTH, DN_HEADS), f32, math.log(1e-3), math.log(1e-1)))
    return {
        "x": jax.random.normal(ks[0], (BATCH, SEQ, D_MODEL), f32),
        "norm1": gain(ks[1], (DEPTH, D_MODEL)),
        "w_in": jax.random.normal(ks[2], (DEPTH, D_MODEL, D_IN_PROJ), f32) * D_MODEL ** -0.5,
        "sb_gain": gain(ks[3], (DEPTH, SB_HEAD_DIM)),
        "dn_conv": jax.random.normal(ks[4], (DEPTH, DN_CONV, 3 * DN_WIDTH), f32) * DN_CONV ** -0.5,
        "dn_a_log": jnp.log(jax.random.uniform(ks[5], (DEPTH, DN_HEADS), f32, 1.0, 16.0)),
        "dn_dt_bias": dt + jnp.log(-jnp.expm1(-dt)),
        "dn_gain": gain(ks[7], (DEPTH, DN_HEAD_DIM)),
        "hg_lb_logits": 0.1 * jax.random.normal(ks[8], (DEPTH, HG_KEY_WIDTH), f32),
        "hg_gain": gain(ks[9], (DEPTH, HG_VAL_DIM)),
        "w_out": jax.random.normal(ks[10], (DEPTH, D_MIX, D_MODEL), f32) * D_MIX ** -0.5,
        "norm2": gain(ks[11], (DEPTH, D_MODEL)),
        "w_gate": jax.random.normal(ks[12], (DEPTH, D_MODEL, D_FF), f32) * D_MODEL ** -0.5,
        "w_up": jax.random.normal(ks[13], (DEPTH, D_MODEL, D_FF), f32) * D_MODEL ** -0.5,
        "w_down": jax.random.normal(ks[14], (DEPTH, D_FF, D_MODEL), f32) * D_FF ** -0.5,
        "final_norm": gain(ks[15], (D_MODEL,)),
    }

def reference(x, norm1, w_in, sb_gain, dn_conv, dn_a_log, dn_dt_bias, dn_gain, hg_lb_logits,
              hg_gain, w_out, norm2, w_gate, w_up, w_down, final_norm):
    lbs = jnp.cumsum(jax.nn.softmax(hg_lb_logits.astype(jnp.float32), axis=0), axis=0)
    lbs = lbs - lbs[0:1]
    for l in range(DEPTH):
        x = hybrid_layer(x, norm1[l], w_in[l], sb_gain[l], dn_conv[l], dn_a_log[l], dn_dt_bias[l],
                         dn_gain[l], lbs[l], hg_gain[l], w_out[l], norm2[l], w_gate[l], w_up[l],
                         w_down[l])
    return rms_norm(x, final_norm)


_drawn_inputs = setup_inputs


def setup_inputs(seed=0):
    import zlib

    import numpy as np

    out = dict(_drawn_inputs(seed))
    spreads = {}
    factors = {'norm1': 3.024,
     'sb_gain': 5.097,
     'dn_gain': 7.365,
     'hg_gain': 8.0,
     'norm2': 4.456,
     'final_norm': 2.861}
    for name, (base, spread) in spreads.items():
        noise = np.random.default_rng([zlib.crc32(name.encode()), seed]).standard_normal(out[name].shape)
        drawn = base * np.exp(spread * noise) if base else spread * noise
        out[name] = __import__('jax').numpy.asarray(drawn.astype(out[name].dtype))
    for name, factor in factors.items():
        out[name] = (out[name] * factor).astype(out[name].dtype)
    return out
```

```python
import concourse.bass as bass
from concourse import mybir
from contextlib import ExitStack

F32 = mybir.dt.float32
F32R = mybir.dt.float32r
I32 = mybir.dt.int32
ALU = mybir.AluOpType
ACT = mybir.ActivationFunctionType
AX = mybir.AxisListType
ds = bass.ds

P = 128
HALF = 512
EPS = 1e-6
BASE = 3
LEVELS = 7


def trunk_program(nc, a, out):
    T, D = a["x"].shape[1:]
    F = a["w_gate"].shape[2]
    NT, KT, NF = T // P, D // P, F // P
    SBH = 4
    SBD = a["sb_gain"].shape[1]
    DNH = a["dn_a_log"].shape[1]
    HGD = a["hg_gain"].shape[1]
    SBW, DNW, HGW = SBH * SBD, DNH * P, D // 4
    NC = 3 * DNW // P
    C_DN = 3 * SBW
    C_Z = C_DN + 3 * DNW
    C_AB = C_Z + DNW
    C_HQ = C_AB + 2 * DNH
    C_HF, C_HI, C_HG = C_HQ + HGW, C_HQ + 2 * HGW, C_HQ + 3 * HGW
    def tile_of(kind, j, first, per_pass, at):
        return kind, first + j * P, per_pass * P, at + j * P
    Z_AT, G_AT, I_AT = 3 * DNW, 4 * DNW, 4 * DNW + HGW
    dn = [tile_of("conv", j, C_DN, NC // 2, 0) for j in range(NC // 2)]
    zz = [tile_of("plain", j, C_Z, 2, Z_AT) for j in range(2)]
    SLOTS = [dn[0], zz[0], dn[1], tile_of("plain", 0, C_HI, 1, I_AT), dn[2], tile_of("chan", 0, C_HQ, 1, 0),
             dn[3], zz[1], dn[4], tile_of("plain", 0, C_HG, 1, G_AT), dn[5], tile_of("chan", 0, C_HF, 1, 2)]
    NS = len(SLOTS)
    NH = 2 * NS
    W_AB, W_P1, W_OUT = 6, 7, 7 + 2 * NS
    W_FF = W_OUT + KT
    SB_AT = 4 * DNW + 2 * HGW
    TM = SB_AT + SBW

    UNITS = []
    for hh in range(2):
        for g in range(2):
            blocks = list(range(4 * g + 3, -1, -1))
            for r, m in enumerate(blocks):
                UNITS.append((hh, g, m, max(m - 4 * g, 0) * P, r, len(blocks), m >= 4 * g))
    assert len(UNITS) == NH

    def before(items, k):
        return sum(1 for u in items[:k] if u)
    DIAG = [u[6] for u in UNITS]
    SUMS = [u[4] < u[5] - 1 for u in UNITS]
    STARTS = [u[6] and 0 < u[4] < u[5] - 1 for u in UNITS]
    ENDS = [u[4] == u[5] - 1 for u in UNITS]
    CONV = [SLOTS[k // 2][0] == "conv" for k in range(NH)]
    TOKM = [SLOTS[k // 2][0] != "chan" for k in range(NH)]
    nd, nsum, nstart, nend, nconv, ntok = (sum(v) for v in (DIAG, SUMS, STARTS, ENDS, CONV, TOKM))

    tm_dram = nc.dram_tensor("projected_tm", [T, TM], F32, kind="Internal").ap()
    cm_dram = nc.dram_tensor("projected_cm", [4, P, T], F32, kind="Internal").ap()

    w_in = a["w_in"][0].rearrange("(k p) n -> p k n", p=P)
    w_out = a["w_out"][0].rearrange("(k p) n -> p k n", p=P)
    w_gate = a["w_gate"][0].rearrange("(k p) n -> p k n", p=P)
    w_up = a["w_up"][0].rearrange("(k p) n -> p k n", p=P)
    w_down = a["w_down"][0].rearrange("(f p) n -> p f n", p=P)
    x_rows = a["x"][0].rearrange("(t p) d -> p t d", p=P)
    out_rows = out[0].rearrange("(t p) d -> p t d", p=P)

    with ExitStack() as ctx:
        sems = {}

        def sem(name):
            sems[name] = ctx.enter_context(nc.semaphore(name))

        def sb(name, shape, dt=F32):
            return ctx.enter_context(nc.sbuf_tensor(name, shape, dt))

        act_h = sb("act_h", [P, KT, T], F32R)
        act_l = sb("act_l", [P, KT, T], F32R)
        w_h = sb("w_h", [P, 2, KT, P], F32R)
        w_l = sb("w_l", [P, 2, KT, P], F32R)
        ff_h = sb("ff_h", [P, 2, T], F32R)
        ff_l = sb("ff_l", [P, 2, T], F32R)
        w_raw = sb("w_raw", [P, 2, KT, P])
        ident = sb("ident", [P, P])
        upto = sb("upto", [P, P])
        ones = sb("ones", [P, P])
        neg_after = sb("neg_after", [P, P])
        neg_ones = sb("neg_ones", [P, P])
        earlier = sb("earlier", [P, P])
        not_earlier = sb("not_earlier", [P, P])
        zeros = sb("zeros", [P, P])
        row_mask = sb("row_mask", [P, LEVELS - 1, 64])
        col_mask = sb("col_mask", [P, LEVELS, 64])
        pair_mask = sb("pair_mask", [P, LEVELS + 1, P])
        head_mask = sb("head_mask", [P, P])
        gain_row = sb("gain_row", [P, D])
        ssq = sb("ssq", [P, NT])
        lnv = sb("lnv", [P, NT])
        eps_col = sb("eps_col", [P, 1])
        rstd = sb("rstd", [P, NT])
        ab_tm = sb("ab_tm", [P, NT, 2 * DNH])
        small = {n: sb(n, [P, NT, DNH]) for n in ("g_all", "beta", "gc", "rest", "whole", "eg", "neg_be")}
        g_all, beta, gc, rest, whole, eg, neg_be = small.values()
        ab_s = sb("ab_s", [P, NT, 2 * DNH])
        dt_row, rate_log, rate = sb("dt_row", [P, DNH]), sb("rate_log", [P, DNH]), sb("rate", [P, DNH])
        r8, r16, r4 = sb("r8", [P, 2 * DNH]), sb("r16", [P, 16]), sb("r4", [P, DNH])
        AREA = 22096
        area = sb("area", [P, AREA])

        def carver():
            at = [0]

            def carve(*shape):
                n = 1
                for s in shape:
                    n *= s
                v = area[:, at[0]:at[0] + n]
                at[0] += n
                assert at[0] <= AREA, (at[0] / 256)
                if len(shape) == 2:
                    v = v.rearrange("p (a b) -> p a b", b=shape[1])
                if len(shape) == 3:
                    v = v.rearrange("p (a b c) -> p a b c", b=shape[1], c=shape[2])
                return v
            return carve

        carve = carver()
        x_sb = carve(NT, D)
        xn = carve(2, D)
        junk = carve(D)
        x_t = carve(2, T)
        gs = x_t[:, 0, :].rearrange("p (a b) -> p a b", a=2)
        ffv = x_t[:, 1, :].rearrange("p (a b) -> p a b", a=2)
        carve = carver()
        sb_t = carve(6, T)
        v_tm = carve(NT, SBW)
        k_one = carve(2, T)
        raw = carve(2, T + 3)
        az = carve(2, HALF)
        sp = carve(2, HALF)
        wt = carve(2, HALF)
        sp_sum = carve(HALF)
        cv = carve(2, HALF)
        cs = carve(2, HALF)
        cact = carve(2, HALF)
        tm_stage = carve(2, 4, P)
        ab_t = cv[:, :, :].rearrange("p a b -> p (a b)")
        cw_rows = carve(P)
        cw = carve(4, NC)
        o_stage = carve(2, 4, SBD)
        carve = carver()
        pin = carve(TM)
        qk = pin[:, 0:2 * DNW].rearrange("p (h c) -> p h c", c=P)
        qn, kn = qk[:, 0:DNH, :], qk[:, DNH:, :]
        vv = pin[:, 2 * DNW:3 * DNW].rearrange("p (h c) -> p h c", c=P)
        cin = carve(4, P)
        kb, kd, qd = (carve(DNH, P) for _ in range(3))
        kt, kbt, qt, qdt = (carve(DNH, P) for _ in range(4))
        span, dtr = carve(DNH, P), carve(DNH, P)
        mm_, mt, at = (carve(DNH, P) for _ in range(3))
        tb = carve(2 * DNH, P).rearrange("p (z h) c -> p z h c", z=2)
        xy = carve(2 * DNH, 64).rearrange("p (z h) c -> p z h c", z=2)
        state = carve(DNH, P)
        hls, hq, hk, hb = carve(4, P), carve(2, P), carve(2, P), carve(2, P)
        el = carve(8, P).rearrange("p (n g) c -> p n g c", g=2)
        qe = carve(8, P).rearrange("p (n g) c -> p n g c", g=2)
        ke = carve(8, P).rearrange("p (n g) c -> p n g c", g=2)
        sc = carve(4, P)
        qb, eb, kdc, kdt, hstate, htmp = (carve(2, P) for _ in range(6))
        gate, sq, mix = carve(D), carve(D), carve(D)
        banks = [ctx.enter_context(nc.psum_tensor(f"banks{i}", [P, 2, HALF], F32)) for i in range(4)]

        def bank(n):
            return banks[n // 2][:, n % 2, :]

        for name in ("consts", "gain_loaded", "small_loaded", "norm_ssq", "norm_ln", "norm_rstd", "norm_xn",
                     "norm_turned", "norm_h", "norm_l", "w_loaded0", "w_loaded1", "wh_ready", "wl_ready", "dense_done", "dense_evac",
                     "k_one_ready", "small_turned", "small_ready"):
            sem(name)
        for name in ("z_done", "z_abs", "z_exp", "z_ln", "sp_ready", "sp_masked", "sum_ready", "tri_done", "wt_ready",
                     "wt_masked", "av_done", "o_evac", "conv_step", "conv_done", "conv_abs", "conv_exp", "conv_ln", "conv_ls", "conv_sg",
                     "conv_act", "tm_turned", "tm_ready", "tm_stored0", "tm_stored1", "cm_stored", "sum_started", "k_zero"):
            sem(name)
        for n in range(NT // 2):
            sem(f"x_loaded{n}")

        def hold(e, n):
            e.tensor_copy(held[:, n:n + 1], eps_col[:, :])

        for name in """rows_loaded gains_loaded o_stored0 o_stored1 pin_loaded cin_loaded zeroed decay_dve decay_act
                decay_sums gup gr_done turned turned_copy kk_done x_done xy d_done tt h_p ks_done kdt_done ho_done vn_done hs_done
                o_done su_done mt_done sq h_abs h_exp h_ln dn_ssq dn_ln dn_r zg_abs zg_exp zg_ln h_ls h_sq h_k0 h_k a_min a_max
                dt dd h_b h_eb h_kd0 h_kd1 h_dl h_dabs h_el zg_ls zg_sg kdt mix_hg vn mix_dn mix_sb msq m_sums m_ln m_r
                act_high act_low t_init vb kd h_q h_qb h_kd at at0 h_ke gated hs_dec s_dec m_n fin dn_rq qkn kb qd a1 h_qe
                h_sc m mt ks r htmp hs_new s_new x_turned x1_ready gu_done ff_silu ff_mul ff_high ff_low down_done x_added
                out_ready out_stored""".split():
            sem(name)

        def absolute_value(e, dst, src):
            return e.tensor_scalar(dst.bitcast(I32), src.bitcast(I32), 0x7fffffff, None, ALU.bitwise_and)

        block = ctx.enter_context(nc.Block())

        def load_tile(e, w, b, src):
            e.wait_ge(sems["wl_ready"], BASE + w - 1)
            e.dma_start(w_raw[:, b], src).then_inc(sems[f"w_loaded{b}"], 16)

        def split_high(e, w, b, used=True):
            e.wait_ge(sems[f"w_loaded{b}"], BASE + 8 * (w - b) + 16)
            if used:
                e.wait_ge(sems["dense_done"], BASE + 2 * (w - 1))
            e.activation(w_h[:, b], w_raw[:, b], ACT.Copy).then_inc(sems["wh_ready"], 1)

        def split_low(e, w, b):
            e.wait_ge(sems["wh_ready"], BASE + w + 1)
            e.tensor_tensor(w_l[:, b], w_raw[:, b], w_h[:, b].bitcast(F32), ALU.subtract).then_inc(sems["wl_ready"], 1)

        def dense_half(e, w, b, th, dst):
            if th == 0:
                e.wait_ge(sems["wl_ready"], BASE + w + 1)
            e.wait_ge(sems["dense_evac"], BASE + 2 * w + th - 1)
            cols = slice(th * HALF, (th + 1) * HALF)
            for k in range(KT):
                e.matmul(dst, w_h[:, b, k], act_h[:, k, cols], start=(k == 0), stop=False)
                e.matmul(dst, w_h[:, b, k], act_l[:, k, cols], start=False, stop=False)
                mm = e.matmul(dst, w_l[:, b, k], act_h[:, k, cols], start=False, stop=(k == KT - 1))
            mm.then_inc(sems["dense_done"], 1)

        def norm_act(e, which):
            for n in range(NT):
                if which == 0:
                    e.wait_ge(sems[f"x_loaded{n // 2}"], BASE + 16)
                else:
                    e.wait_ge(sems["x1_ready"], BASE + 2 * KT)
                e.activation(junk, x_sb[:, n, :], ACT.Square, accum_out=ssq[:, n:n + 1]).then_inc(sems["norm_ssq"], 1)
                e.wait_ge(sems["norm_ssq"], BASE + which * NT + n + 1)
                e.activation(lnv[:, n:n + 1], ssq[:, n:n + 1], ACT.Ln, scale=1.0 / D, bias=eps_col[:, 0:1]).then_inc(sems["norm_ln"], 1)
                e.wait_ge(sems["norm_ln"], BASE + which * NT + n + 1)
                e.activation(rstd[:, n:n + 1], lnv[:, ds(n, 1)], ACT.Exp, scale=-0.5).then_inc(sems["norm_rstd"], 1)
            with e.Fori(0, NT // 2) as i:
                for b in range(2):
                    n = 2 * i + b
                    e.wait_ge(sems["norm_turned"], BASE + which * NT + n + 1)
                    e.activation(act_h[:, :, ds(n * P, P)], banks[b][:, :, :].rearrange("p a (k c) -> p (a k) c", c=P),
                                      ACT.Copy).then_inc(sems["norm_h"], 1)

        def norm_dve(e, which):
            e.wait_ge(sems["gain_loaded"], BASE + 16 * (which + 1))
            def scaled(n, b):
                e.wait_ge(sems["norm_rstd"], BASE + which * NT + n + 1)
                e.wait_ge(sems["norm_turned"], BASE + which * NT + n - 1)
                e.scalar_tensor_tensor(out=xn[:, b], in0=x_sb[:, n, :], scalar=rstd[:, ds(n, 1)], in1=gain_row[:, :],
                                            op0=ALU.mult, op1=ALU.mult).then_inc(sems["norm_xn"], 1)

            def low(n, b):
                e.wait_ge(sems["norm_h"], BASE + which * NT + n + 1)
                e.tensor_tensor(act_l[:, :, ds(n * P, P)], banks[b][:, :, :].rearrange("p a (k c) -> p (a k) c", c=P),
                                     act_h[:, :, ds(n * P, P)].bitcast(F32), ALU.subtract).then_inc(sems["norm_l"], 1)
            with e.Fori(0, NT // 2) as i:
                for b in range(2):
                    scaled(2 * i + b, b)
                for b in range(2):
                    low(2 * i + b, b)

        def norm_pe(e, which):
            with e.Fori(0, NT // 2) as i:
                for b in range(2):
                    n = 2 * i + b
                    e.wait_ge(sems["norm_xn"], BASE + which * NT + n + 1)
                    e.wait_ge(sems["norm_l"], BASE + which * NT + n - 1)
                    for k in range(KT):
                        mm = e.transpose(banks[b][:, k // 4, (k % 4) * P:(k % 4 + 1) * P], xn[:, b, k * P:(k + 1) * P], ident[:, :])
                    mm.then_inc(sems["norm_turned"], 1)

        held = sb("held", [P, 8])

        def masks(e):
            for name in sems:
                if name != "consts":
                    e.sem_inc(sems[name], BASE)
            cleared = 0

            def select(v, op, base, pattern, cm, fill):
                nonlocal cleared
                cleared += 1
                e.wait_ge(sems["consts"], cleared)
                e.affine_select(out=v, in_=v, compare_op=op, fill=fill, base=base, pattern=pattern, channel_multiplier=cm).then_inc(sems["consts"], 1)

            for v, value in ((ident, 0.0), (upto, 1.0), (neg_after, -1.0), (ones, 1.0), (earlier, 1.0), (not_earlier, 1.0), (zeros, 0.0), (neg_ones, -1.0), (row_mask, 1.0),
                             (col_mask, 1.0), (pair_mask, 1.0), (head_mask, 1.0), (eps_col, EPS)):
                cleared += 1
                e.memset(v[:], value).then_inc(sems["consts"], 1)
            cleared -= 1
            select(ident[:, :], ALU.not_equal, 0, [[1, P]], -1, 1.0)
            select(upto[:, :], ALU.is_ge, 0, [[1, P]], -1, 0.0)
            select(earlier[:, :], ALU.is_gt, 0, [[1, P]], -1, 0.0)
            select(not_earlier[:, :], ALU.is_ge, 0, [[-1, P]], 1, 0.0)
            select(neg_after[:, :], ALU.is_ge, 0, [[-1, P]], 1, 0.0)
            for lv in range(LEVELS):
                s = 2 ** lv
                if lv < LEVELS - 1:
                    m = row_mask[:, lv, :].rearrange("p (b r) -> p b r", r=s)
                    select(m, ALU.is_ge, -s, [[-2 * s, 64 // s], [0, s]], 1, 0.0)
                    select(m, ALU.is_ge, 2 * s - 1, [[2 * s, 64 // s], [0, s]], -1, 0.0)
                m = col_mask[:, lv, :].rearrange("p (b r) -> p b r", r=s)
                select(m, ALU.is_ge, 0, [[-2 * s, 64 // s], [0, s]], 1, 0.0)
                select(m, ALU.is_ge, s - 1, [[2 * s, 64 // s], [0, s]], -1, 0.0)
            for lv in range(LEVELS):
                h = P >> (lv + 1)
                m = pair_mask[:, lv, :].rearrange("p (b r) -> p b r", r=2 * h)
                nb = P // (2 * h)
                select(m, ALU.is_ge, -h, [[0, nb], [1, 2 * h]], 0, 0.0)
                select(m, ALU.is_ge, 0, [[-2 * h, nb], [0, 2 * h]], 1, 0.0)
                select(m, ALU.is_ge, h - 1, [[2 * h, nb], [0, 2 * h]], -1, 0.0)
            select(pair_mask[:, LEVELS, :], ALU.is_equal, 0, [[1, P]], -1, 0.0)
            m = head_mask[:, :].rearrange("p (b r) -> p b r", r=64)
            select(m, ALU.is_ge, 0, [[-64, 2], [0, 64]], 1, 0.0)
            select(m, ALU.is_ge, 63, [[64, 2], [0, 64]], -1, 0.0)
            return cleared + 1

        def in_tile(w):
            return w_in[:, :, ds(w * P, P)]

        def first_sync(e):
            with e.Fori(0, 3) as i:
                for b in range(2):
                    load_tile(e, 2 * i + b, b, in_tile(2 * i + b))
            load_tile(e, W_AB, 0, w_in[:, :, C_AB:C_AB + P])

        def first_pe(e):
            e.wait_ge(sems["small_loaded"], BASE + 16)
            e.transpose(bank(7)[:, 0:4 * NC], cw_rows[0:4 * NC, :], ident[0:4 * NC, 0:4 * NC]).then_inc(sems["small_turned"], 1)
            with e.Fori(0, 3) as i:
                for b in range(2):
                    for th in range(2):
                        dense_half(e, 2 * i + b, b, th, bank(th))
            for th in range(2):
                dense_half(e, W_AB, 0, th, bank(th))
            for v in range(2):
                for th in range(2):
                    n = 2 * v + th
                    e.wait_ge(sems["dense_evac"], BASE + 2 * (4 + v) + th + 1)
                    if n >= 2:
                        e.wait_ge(sems["small_ready"], BASE + n)
                    for j in range(4):
                        mm = e.transpose(bank(2 + n % 2)[:, j * P:(j + 1) * P],
                                         sb_t[:, 4 + v, (4 * th + j) * P:(4 * th + j + 1) * P], ident[:, :])
                    mm.then_inc(sems["small_turned"], 1)
            e.wait_ge(sems["dense_evac"], BASE + 2 * W_AB + 2)
            for t in range(NT):
                mm = e.transpose(bank(4)[:, 8 * t:8 * t + 8], ab_t[0:8, t * P:(t + 1) * P], ident[0:8, 0:8])
            mm.then_inc(sems["small_turned"], 1)

        def first_act(e):
            split_high(e, 0, 0)
            with e.Fori(0, 3) as i:
                for b in range(2):
                    w = 2 * i + b
                    split_high(e, w + 1, 1 - b)
                    for th in range(2):
                        e.wait_ge(sems["dense_done"], BASE + 2 * w + th + 1)
                        e.activation(sb_t[:, w, th * HALF:(th + 1) * HALF], bank(th), ACT.Copy).then_inc(sems["dense_evac"], 1)
            split_high(e, W_P1, 1)
            for th in range(2):
                e.wait_ge(sems["dense_done"], BASE + 2 * W_AB + th + 1)
                e.activation(ab_t[0:8, th * HALF:(th + 1) * HALF], bank(th)[0:8, :], ACT.Copy).then_inc(sems["dense_evac"], 1)

        def first_pool(e):
            e.wait_ge(sems["norm_l"], BASE + NT)
            e.memset(k_one[:, :, :], 0.0).then_inc(sems["k_zero"], 1)
            e.memset(raw[:, :, 0:3], 0.0).then_inc(sems["k_zero"], 1)
            split_low(e, 0, 0)
            with e.Fori(0, 3) as i:
                for b in range(2):
                    split_low(e, 2 * i + b + 1, 1 - b)
            split_low(e, W_P1, 1)

        def first_dve(e):
            e.wait_ge(sems["small_turned"], BASE + 1)
            e.tensor_copy(cw[:, :, :], bank(7)[:, 0:4 * NC].rearrange("p (k c) -> p k c", c=NC)).then_inc(sems["small_ready"], 1)
            for v in range(2):
                for th in range(2):
                    n = 2 * v + th
                    e.wait_ge(sems["small_turned"], BASE + n + 2)
                    e.tensor_copy(v_tm[:, 4 * th:4 * th + 4, v * P:(v + 1) * P],
                                       bank(2 + n % 2).rearrange("p (t c) -> p t c", c=P)).then_inc(sems["small_ready"], 1)
            e.wait_ge(sems["small_turned"], BASE + 6)
            e.tensor_copy(ab_tm[:, :, :], bank(4)[:, 0:8 * NT].rearrange("p (t c) -> p t c", c=8)).then_inc(sems["small_ready"], 1)

        Z = [bank(2), bank(3)]
        O, TURN = bank(4), [bank(5), bank(6)]
        Ov = O[:, 0:4 * SBD].rearrange("p (j d) -> p j d", d=SBD)

        def lead_sync(e):
            with e.Fori(0, 2) as i:
                for s, (kind, col, per, at) in enumerate(SLOTS):
                    w = W_P1 + NS * i + s
                    load_tile(e, w, (W_P1 + s) % 2, w_in[:, :, ds(per * i + col, P)])

        def mix_pe(e):
            e.wait_ge(sems["small_ready"], BASE + 6)
            with e.Fori(0, 2) as i:
                def scores(k):
                    hh, g, m, c0, r, R, diag = UNITS[k]
                    if r == 0 and g == 0:
                        e.wait_ge(sems["k_one_ready"], BASE + 2 * i + hh + 1)
                    e.wait_ge(sems["wt_ready"], BASE + NH * i + k - 1)
                    e.matmul(Z[k % 2][:, c0:], k_one[:, hh, m * P:(m + 1) * P],
                                  sb_t[:, i, g * HALF + c0:(g + 1) * HALF], start=True, stop=True).then_inc(sems["z_done"], 1)

                def suffix(k):
                    hh, g, m, c0, r, R, diag = UNITS[k]
                    if diag:
                        e.wait_ge(sems["sp_masked"], BASE + nd * i + before(DIAG, k) + 1)
                    else:
                        e.wait_ge(sems["sp_ready"], BASE + NH * i + k + 1)
                    if r > 0:
                        e.wait_ge(sems["sum_ready"], BASE + nsum * i + before(SUMS, k))
                        c = c0 + P if diag else c0
                        e.matmul(Z[k % 2][:, c:], neg_ones[:, :], sp_sum[:, c:], start=False, stop=True,
                                 skip_group_check=True)
                    e.matmul(Z[k % 2][:, c0:], neg_after[:, :], sp[:, k % 2, c0:], start=False, stop=True,
                                  skip_group_check=True).then_inc(sems["tri_done"], 1)

                def weigh(k):
                    hh, g, m, c0, r, R, diag = UNITS[k]
                    if diag:
                        e.wait_ge(sems["wt_masked"], BASE + nd * i + before(DIAG, k) + 1)
                    else:
                        e.wait_ge(sems["wt_ready"], BASE + NH * i + k + 1)
                    if r == 0:
                        e.wait_ge(sems["o_evac"], BASE + nend * i + before(ENDS, k))
                    for j in range(c0 // P, 4):
                        mm = e.matmul(Ov[:, j, :], wt[:, k % 2, j * P:(j + 1) * P], v_tm[:, m, ds(i * P + hh * SBD, SBD)],
                                      start=(r == 0), stop=(r == R - 1), skip_group_check=True)
                    mm.then_inc(sems["av_done"], 1)

                def turn(k):
                    n = ntok * i + before(TOKM, k)
                    e.wait_ge(sems["tm_ready"], BASE + n - 1)
                    if CONV[k]:
                        e.wait_ge(sems["conv_act"], BASE + nconv * i + before(CONV, k) + 1)
                        src = cact[:, k % 2, :]
                    else:
                        e.wait_ge(sems["dense_evac"], BASE + 2 * W_P1 + NH * i + k + 1)
                        src = raw[:, k // 2 % 2, 3 + (k % 2) * HALF:3 + (k % 2 + 1) * HALF]
                    for j in range(4):
                        mm = e.transpose(TURN[k % 2][:, j * P:(j + 1) * P], src[:, j * P:(j + 1) * P], ident[:, :])
                    mm.then_inc(sems["tm_turned"], 1)

                for k in range(NH + 2):
                    if k < NH:
                        scores(k)
                        dense_half(e, W_P1 + NS * i + k // 2, (W_P1 + k // 2) % 2, k % 2, bank(k % 2))
                        suffix(k)
                    if 1 <= k <= NH:
                        weigh(k - 1)
                    if k >= 2 and TOKM[k - 2]:
                        turn(k - 2)

        def mix_act(e):
            e.wait_ge(sems["k_zero"], BASE + 2)
            with e.Fori(0, 2) as i:
                for hh in range(2):
                    e.wait_ge(sems["z_done"], BASE + NH * i)
                    rows = slice(hh * SBD, (hh + 1) * SBD)
                    e.activation(k_one[rows, hh, :], sb_t[rows, 2 + i, :], ACT.Copy, scale=SBD ** -0.5).then_inc(sems["k_one_ready"], 1)

                def take(k):
                    w0 = 2 * W_P1 + NH * i + k
                    s = k // 2
                    e.wait_ge(sems["dense_done"], BASE + w0 + 1)
                    e.wait_ge(sems["cm_stored"], BASE + 16 * (2 * i + sum(u[0] == "chan" for u in SLOTS[:max(s - 1, 0)])))
                    e.wait_ge(sems["conv_done"], BASE + nconv * i + before(CONV, 2 * max(s - 1, 0)))
                    e.wait_ge(sems["tm_turned"], BASE + ntok * i + before(TOKM, 2 * max(s - 1, 0)))
                    e.activation(raw[:, s % 2, 3 + (k % 2) * HALF:3 + (k % 2 + 1) * HALF], bank(k % 2), ACT.Copy).then_inc(sems["dense_evac"], 1)

                def store_chan(k):
                    s = k // 2
                    e.wait_ge(sems["dense_evac"], BASE + 2 * W_P1 + NH * i + k + 1)
                    e.dma_start(cm_dram[ds(i + SLOTS[s][3], 1), :, :].rearrange("a p t -> p (a t)"),
                                     raw[:, s % 2, 3:3 + T]).then_inc(sems["cm_stored"], 16)

                def z_soft(k):
                    hh, g, m, c0, r, R, diag = UNITS[k]
                    n = NH * i + k
                    e.wait_ge(sems["z_abs"], BASE + n + 1)
                    e.activation(az[:, k % 2, c0:], az[:, k % 2, c0:], ACT.Exp, scale=-1.0).then_inc(sems["z_exp"], 1)
                    e.wait_ge(sems["z_exp"], BASE + n + 1)
                    e.activation(az[:, k % 2, c0:], az[:, k % 2, c0:], ACT.Ln, bias=1.0).then_inc(sems["z_ln"], 1)

                def weights(k):
                    c0 = UNITS[k][3]
                    n = NH * i + k
                    e.wait_ge(sems["tri_done"], BASE + n + 1)
                    e.wait_ge(sems["av_done"], BASE + n - 1)
                    e.activation(wt[:, k % 2, c0:], Z[k % 2][:, c0:], ACT.Exp).then_inc(sems["wt_ready"], 1)

                def store_tok(k):
                    n = ntok * i + before(TOKM, k)
                    kind, col, per, at = SLOTS[k // 2]
                    step = (NC // 2) * P if kind == "conv" else per
                    e.wait_ge(sems["tm_ready"], BASE + n + 1)
                    e.dma_start(tm_dram[(k % 2) * HALF:(k % 2 + 1) * HALF, ds(step * i + at, P)]
                                     .rearrange("(j p) c -> p j c", p=P), tm_stage[:, k % 2]).then_inc(sems[f"tm_stored{k % 2}"], 16)

                def store_out(k):
                    hh, g = UNITS[k][:2]
                    n = before(ENDS, k)
                    e.wait_ge(sems["o_evac"], BASE + nend * i + n + 1)
                    e.dma_start(tm_dram[g * HALF:(g + 1) * HALF, ds(i * P + SB_AT + hh * SBD, SBD)]
                                     .rearrange("(j p) c -> p j c", p=P), o_stage[:, n % 2]).then_inc(sems[f"o_stored{n % 2}"], 16)

                def silu(k):
                    n = nconv * i + before(CONV, k)
                    e.wait_ge(sems["conv_abs"], BASE + n + 1)
                    e.activation(cs[:, k % 2, :], cs[:, k % 2, :], ACT.Exp, scale=-1.0).then_inc(sems["conv_exp"], 1)
                    e.wait_ge(sems["conv_exp"], BASE + n + 1)
                    e.activation(cs[:, k % 2, :], cs[:, k % 2, :], ACT.Ln, bias=1.0).then_inc(sems["conv_ln"], 1)
                    e.wait_ge(sems["conv_ls"], BASE + n + 1)
                    e.activation(cs[:, k % 2, :], cs[:, k % 2, :], ACT.Exp).then_inc(sems["conv_sg"], 1)

                for k in range(NH + 5):
                    if 1 <= k <= NH:
                        take(k - 1)
                    if k < NH:
                        z_soft(k)
                        if k % 2 == 0:
                            split_high(e, W_P1 + NS * i + k // 2 + 1, (W_P1 + k // 2 + 1) % 2)
                    if 1 <= k <= NH:
                        weights(k - 1)
                        if not TOKM[k - 1] and k % 2 == 0:
                            store_chan(k - 1)
                    if 4 <= k < NH + 4 and TOKM[k - 4]:
                        store_tok(k - 4)
                    if 3 <= k < NH + 3 and ENDS[k - 3]:
                        store_out(k - 3)
                    if 1 <= k <= NH and CONV[k - 1]:
                        silu(k - 1)

        def mixed_to_dram(e):
            e.wait_ge(sems["cm_stored"], BASE + 16 * 4)
            for half in range(2):
                e.wait_ge(sems[f"tm_stored{half}"], BASE + 16 * ntok)
                e.wait_ge(sems[f"o_stored{half}"], BASE + 16 * nend)
            e.wait_ge(sems["av_done"], BASE + 2 * NH)

        def mix_pool(e):
            with e.Fori(0, 2) as i:
                def mask_sp(k):
                    hh, g, m, c0, r, R, diag = UNITS[k]
                    e.wait_ge(sems["sp_ready"], BASE + NH * i + k + 1)
                    e.tensor_tensor(sp[:, k % 2, c0:c0 + P], sp[:, k % 2, c0:c0 + P], earlier[:, :], ALU.mult).then_inc(sems["sp_masked"], 1)

                def add_sum(k):
                    hh, g, m, c0, r, R, diag = UNITS[k]
                    n = nsum * i + before(SUMS, k)
                    e.wait_ge(sems["tri_done"], BASE + NH * i + k + 1)
                    if diag:
                        e.wait_ge(sems["sp_masked"], BASE + nd * i + before(DIAG, k) + 1)
                        new = e.tensor_tensor(sp_sum[:, c0:c0 + P], sp[:, k % 2, c0:c0 + P], ones[:, :], ALU.mult)
                        if r == 0:
                            new.then_inc(sems["sum_ready"], 1)
                            return
                        new.then_inc(sems["sum_started"], 1)
                        c0 += P
                        e.wait_ge(sems["sum_started"], BASE + nstart * i + before(STARTS, k) + 1)
                    e.wait_ge(sems["sum_ready"], BASE + n)
                    e.tensor_tensor(sp_sum[:, c0:], sp_sum[:, c0:], sp[:, k % 2, c0:], ALU.add).then_inc(sems["sum_ready"], 1)

                for k in range(NH):
                    if True:
                        if k % 2 == 0:
                            split_low(e, W_P1 + NS * i + k // 2 + 1, (W_P1 + k // 2 + 1) % 2)
                        if DIAG[k]:
                            mask_sp(k)
                        if SUMS[k]:
                            add_sum(k)

        def mix_dve(e):
            with e.Fori(0, 2) as i:
                def absolute(k):
                    hh, g, m, c0, r, R, diag = UNITS[k]
                    e.wait_ge(sems["z_done"], BASE + NH * i + k + 1)
                    e.wait_ge(sems["sp_ready"], BASE + NH * i + k - 1)
                    absolute_value(e, az[:, k % 2, c0:], Z[k % 2][:, c0:]).then_inc(sems["z_abs"], 1)

                def softplus(k):
                    hh, g, m, c0, r, R, diag = UNITS[k]
                    n = NH * i + k
                    e.wait_ge(sems["z_ln"], BASE + n + 1)
                    e.wait_ge(sems["tri_done"], BASE + n - 1)
                    if k >= 2 and SUMS[k - 2]:
                        e.wait_ge(sems["sum_ready"], BASE + nsum * i + before(SUMS, k - 1))
                    e.scalar_tensor_tensor(out=sp[:, k % 2, c0:], in0=Z[k % 2][:, c0:], scalar=0.0, in1=az[:, k % 2, c0:],
                                                op0=ALU.max, op1=ALU.add).then_inc(sems["sp_ready"], 1)

                def convolve(k):
                    s = k // 2
                    n = nconv * i + before(CONV, k)
                    ch = (NC // 2) * i + (SLOTS[s][1] - C_DN) // P
                    at = (k % 2) * HALF
                    e.wait_ge(sems["dense_evac"], BASE + 2 * W_P1 + NH * i + k + 1)
                    e.wait_ge(sems["conv_act"], BASE + n - 1)
                    e.tensor_scalar(cv[:, k % 2], raw[:, s % 2, at + 3:at + 3 + HALF], cw[:, 3, ds(ch, 1)], None, ALU.mult).then_inc(sems["conv_step"], 1)
                    for tap in range(2, -1, -1):
                        e.wait_ge(sems["conv_step"], BASE + 3 * n + 3 - tap)
                        ins = e.scalar_tensor_tensor(out=cv[:, k % 2], in0=raw[:, s % 2, at + tap:at + tap + HALF],
                                                     scalar=cw[:, tap, ds(ch, 1)], in1=cv[:, k % 2], op0=ALU.mult, op1=ALU.add)
                        ins.then_inc(sems["conv_step" if tap else "conv_done"], 1)

                def conv_abs(k):
                    n = nconv * i + before(CONV, k)
                    e.wait_ge(sems["conv_done"], BASE + n + 1)
                    absolute_value(e, cs[:, k % 2, :], cv[:, k % 2, :]).then_inc(sems["conv_abs"], 1)

                def conv_gate(k):
                    n = nconv * i + before(CONV, k)
                    e.wait_ge(sems["conv_ln"], BASE + n + 1)
                    e.scalar_tensor_tensor(out=cs[:, k % 2], in0=cv[:, k % 2], scalar=0.0, in1=cs[:, k % 2],
                                                op0=ALU.min, op1=ALU.subtract).then_inc(sems["conv_ls"], 1)

                def conv_silu(k):
                    n = nconv * i + before(CONV, k)
                    e.wait_ge(sems["conv_sg"], BASE + n + 1)
                    e.wait_ge(sems["tm_turned"], BASE + ntok * i + before(TOKM, max(k - 1, 0)))
                    e.tensor_tensor(cact[:, k % 2], cv[:, k % 2], cs[:, k % 2], ALU.mult).then_inc(sems["conv_act"], 1)

                def stage_tok(k):
                    n = ntok * i + before(TOKM, k)
                    e.wait_ge(sems["tm_turned"], BASE + n + 1)
                    e.wait_ge(sems[f"tm_stored{k % 2}"], BASE + 16 * (ntok // 2 * i + before(TOKM, k) // 2))
                    e.tensor_copy(tm_stage[:, k % 2], TURN[k % 2].rearrange("p (j c) -> p j c", c=P)).then_inc(sems["tm_ready"], 1)

                def mask_wt(k):
                    hh, g, m, c0, r, R, diag = UNITS[k]
                    e.wait_ge(sems["wt_ready"], BASE + NH * i + k + 1)
                    hold(e, k % 2)
                    e.copy_predicated(wt[:, k % 2, c0:c0 + P], not_earlier[:, :].bitcast(I32), zeros[:, :]).then_inc(sems["wt_masked"], 1)

                def take_out(k):
                    hh, g, m, c0, r, R, diag = UNITS[k]
                    e.wait_ge(sems["av_done"], BASE + NH * i + k + 1)
                    n = before(ENDS, k)
                    e.wait_ge(sems[f"o_stored{n % 2}"], BASE + 16 * (nend // 2 * i + n // 2))
                    e.tensor_copy(o_stage[:, n % 2], Ov[:, :, :]).then_inc(sems["o_evac"], 1)

                for k in range(NH + 4):
                    if k < NH:
                        absolute(k)
                    if 1 <= k <= NH and DIAG[k - 1]:
                        mask_wt(k - 1)
                    if 1 <= k <= NH and CONV[k - 1]:
                        convolve(k - 1)
                        conv_abs(k - 1)
                    if k < NH:
                        softplus(k)
                    if 3 <= k < NH + 3 and TOKM[k - 3]:
                        stage_tok(k - 3)
                    if 1 <= k <= NH and CONV[k - 1]:
                        conv_gate(k - 1)
                    if 2 <= k <= NH + 1 and ENDS[k - 2]:
                        take_out(k - 2)
                    if 1 <= k <= NH and CONV[k - 1]:
                        conv_silu(k - 1)

        def decay_dve(e):
            e.wait_ge(sems["small_ready"], BASE + 6)
            e.wait_ge(sems["rows_loaded"], BASE + 32)
            e.tensor_tensor(ab_tm[:, :, 0:DNH], ab_tm[:, :, 0:DNH], dt_row[:, :].unsqueeze(1).to_broadcast([P, NT, DNH]),
                                 ALU.add).then_inc(sems["decay_dve"], 1)
            e.wait_ge(sems["decay_dve"], BASE + 1)
            absolute_value(e, ab_s[:, :, :], ab_tm[:, :, :]).then_inc(sems["decay_dve"], 1)
            e.wait_ge(sems["decay_act"], BASE + 3)
            e.scalar_tensor_tensor(out=g_all[:, :, :], in0=ab_tm[:, :, 0:DNH], scalar=0.0, in1=ab_s[:, :, 0:DNH],
                                        op0=ALU.max, op1=ALU.add).then_inc(sems["decay_dve"], 1)
            e.scalar_tensor_tensor(out=beta[:, :, :], in0=ab_tm[:, :, DNH:], scalar=0.0, in1=ab_s[:, :, DNH:],
                                        op0=ALU.min, op1=ALU.subtract).then_inc(sems["decay_dve"], 1)
            e.wait_ge(sems["decay_dve"], BASE + 3)
            e.scalar_tensor_tensor(out=g_all[:, :, :], in0=g_all[:, :, :], scalar=-1.0,
                                        in1=rate[:, :].unsqueeze(1).to_broadcast([P, NT, DNH]), op0=ALU.mult, op1=ALU.mult).then_inc(sems["decay_dve"], 1)
            e.wait_ge(sems["decay_sums"], BASE + 1)
            e.tensor_copy(gc[:, :, :], bank(0)[:, 0:NT * DNH].rearrange("p (t h) -> p t h", h=DNH)).then_inc(sems["decay_dve"], 1)
            e.tensor_copy(rest[:, :, :], bank(0)[:, NT * DNH:2 * NT * DNH].rearrange("p (t h) -> p t h", h=DNH)).then_inc(sems["decay_dve"], 1)
            e.wait_ge(sems["decay_act"], BASE + 5)
            e.wait_ge(sems["decay_dve"], BASE + 7)
            e.tensor_tensor(rest[:, :, :], rest[:, :, :], gc[:, :, :], ALU.subtract).then_inc(sems["decay_dve"], 1)
            e.wait_ge(sems["decay_act"], BASE + 6)
            e.scalar_tensor_tensor(out=neg_be[:, :, :], in0=beta[:, :, :], scalar=-1.0, in1=eg[:, :, :],
                                        op0=ALU.mult, op1=ALU.mult).then_inc(sems["decay_dve"], 1)

        def decay_act(e):
            e.wait_ge(sems["rows_loaded"], BASE + 32)
            e.activation(rate[:, :], rate_log[:, :], ACT.Exp).then_inc(sems["decay_act"], 1)
            e.wait_ge(sems["decay_dve"], BASE + 2)
            e.activation(ab_s[:, :, :], ab_s[:, :, :], ACT.Exp, scale=-1.0).then_inc(sems["decay_act"], 1)
            e.wait_ge(sems["decay_act"], BASE + 2)
            e.activation(ab_s[:, :, :], ab_s[:, :, :], ACT.Ln, bias=1.0).then_inc(sems["decay_act"], 1)
            e.wait_ge(sems["decay_dve"], BASE + 4)
            e.activation(beta[:, :, :], beta[:, :, :], ACT.Exp).then_inc(sems["decay_act"], 1)
            e.wait_ge(sems["decay_dve"], BASE + 7)
            e.activation(whole[:, :, :], rest[:, :, :], ACT.Exp).then_inc(sems["decay_act"], 1)
            e.activation(eg[:, :, :], gc[:, :, :], ACT.Exp).then_inc(sems["decay_act"], 1)
            e.wait_ge(sems["decay_dve"], BASE + 8)
            e.activation(rest[:, :, :], rest[:, :, :], ACT.Exp).then_inc(sems["decay_act"], 1)

        def decay_pe(e):
            e.wait_ge(sems["decay_dve"], BASE + 5)
            e.wait_ge(sems["dense_evac"], BASE + 2 * W_OUT)
            e.wait_ge(sems["tm_ready"], BASE + 2 * ntok)
            e.matmul(bank(0)[:, 0:NT * DNH], upto[:, :], g_all[:, :, :], start=True, stop=True)
            e.matmul(bank(0)[:, NT * DNH:2 * NT * DNH], ones[:, :], g_all[:, :, :], start=True, stop=True).then_inc(sems["decay_sums"], 1)

        def per_head(v, t, n=DNH, width=P):
            return v[:, t, :].unsqueeze(2).to_broadcast([P, n, width])

        def heads(v):
            return v.rearrange("p (h c) -> p h c", c=P)

        def left(v, s):
            return v.rearrange("p h (b z r) -> p (h b) z r", z=2, r=s)[:, :, 0, :]

        def right(v, s):
            return v.rearrange("p h (b z r) -> p (h b) z r", z=2, r=s)[:, :, 1, :]

        def blocks(v, s):
            return v.rearrange("p h (b r) -> p (h b) r", r=s)

        def mask_of(m, lv):
            return m[:, lv, :].unsqueeze(1).to_broadcast([P, DNH, 64])

        NX = 13

        def mixer_sync(e):
            with e.Fori(0, NT) as t:
                e.wait_ge(sems["h_q"], BASE + t)
                e.dma_start(cin[:, :, :], cm_dram[:, :, ds(t * P, P)].rearrange("a p c -> p a c")).then_inc(sems["cin_loaded"], 16)
                e.wait_ge(sems["fin"], BASE + t)
                e.wait_ge(sems["hs_done"], BASE + t)
                e.dma_start(pin[:, :], tm_dram[ds(t * P, P), :]).then_inc(sems["pin_loaded"], 16)

        def mixer_pe(e):
            with e.Fori(0, NT) as t:
                e.wait_ge(sems["gup"], BASE + t + 1)
                e.wait_ge(sems["s_new"], BASE + t)
                e.matmul(bank(7), ones[:, :], span[:, :, :], start=True, stop=True).then_inc(sems["gr_done"], 1)
                free = ("mix_hg", "kdt", "htmp", "act_low")
                for n, (src, name) in enumerate(((kn, "qkn"), (kb, "kb"), (qn, "qkn"), (qd, "qd"))):
                    e.wait_ge(sems[name], BASE + t + 1)
                    e.wait_ge(sems[free[n]], BASE + (2 * t if n == 3 else t))
                    for h in range(DNH):
                        mm = e.transpose(bank(n)[:, h * P:(h + 1) * P], src[:, h, :], ident[:, :])
                    mm.then_inc(sems["turned"], 1)
                e.wait_ge(sems["turned_copy"], BASE + 4 * t + 3)
                e.wait_ge(sems["act_low"], BASE + 2 * t)
                e.wait_ge(sems["vn"], BASE + t)
                e.wait_ge(sems["mix_dn"], BASE + t)
                for n, (lhs, rhs) in enumerate(((kbt, kt), (kt, kbt), (kt, qt))):
                    for h in range(DNH):
                        mm = e.matmul(bank(4 + n)[:, h * P:(h + 1) * P], lhs[:, h, :], rhs[:, h, :], start=True, stop=True)
                    mm.then_inc(sems["kk_done"], 1)

                def pack(lv):
                    s = 2 ** lv
                    e.wait_ge(sems["tt"], BASE + NX * t + 2 * lv)
                    e.wait_ge(sems["turned_copy"], BASE + 4 * t + 4)
                    for h in range(DNH):
                        if lv < LEVELS - 1:
                            e.matmul(bank(2)[:, h * 64:(h + 1) * 64], mt[:, h, :], left(tb[:, 0, h:h + 1, :], s), start=True, stop=True)
                        mm = e.matmul(bank(2)[:, 256 + h * 64:256 + (h + 1) * 64], mm_[:, h, :], right(tb[:, 1, h:h + 1, :], s),
                                      start=True, stop=True)
                    mm.then_inc(sems["x_done"], 1)

                def update(lv):
                    e.wait_ge(sems["xy"], BASE + (NX * t + 2 * lv + (2 if lv < LEVELS - 1 else 1)))
                    for h in range(DNH):
                        if lv < LEVELS - 1:
                            e.matmul(bank(3)[:, h * 64:(h + 1) * 64], tb[:, 1, h, :], xy[:, 0, h, :], start=True, stop=True)
                        mm = e.matmul(bank(3)[:, 256 + h * 64:256 + (h + 1) * 64], tb[:, 0, h, :], xy[:, 1, h, :], start=True, stop=True)
                    mm.then_inc(sems["d_done"], 1)

                def scores(lv):
                    e.wait_ge(sems["h_qe"], BASE + 2 * t + lv // 4 + 1)
                    e.wait_ge(sems["h_ke"], BASE + 2 * t + lv // 4 + 1)
                    if lv >= 2:
                        e.wait_ge(sems["h_sc"], BASE + 8 * t + lv - 1)
                    if lv == 1:
                        e.wait_ge(sems["at0"], BASE + t + 1)
                    for h in range(4):
                        rows = slice(h % 2 * 64, h % 2 * 64 + 64)
                        mm = e.matmul(banks[3 * (lv % 2)][:, h % 2, h // 2 * P:(h // 2 + 1) * P], ke[rows, lv % 4, h // 2, :],
                                      qe[rows, lv % 4, h // 2, :], start=True, stop=True)
                    mm.then_inc(sems["h_p"], 1)

                pack(1); scores(0); update(1); scores(1)
                pack(2); scores(2); update(2); scores(3)
                e.wait_ge(sems["s_new"], BASE + t)
                for h in range(DNH):
                    mm = e.matmul(bank(4)[:, h * P:(h + 1) * P], kt[:, h, :], state[:, h, :], start=True, stop=True)
                mm.then_inc(sems["ks_done"], 1)
                pack(3); update(3)
                pack(4); scores(4); update(4); scores(5)
                pack(5); scores(6); update(5); scores(7)
                pack(6)
                e.wait_ge(sems["h_sc"], BASE + 8 * t + 8)
                e.wait_ge(sems["h_kd"], BASE + t + 1)
                for g in range(2):
                    mm = e.transpose(bank(1)[:, g * P:(g + 1) * P], kdc[:, g, :], ident[:, :])
                mm.then_inc(sems["kdt_done"], 1)
                update(6)
                e.wait_ge(sems["h_qb"], BASE + t + 1)
                e.wait_ge(sems["hs_new"], BASE + t)
                for g in range(2):
                    e.matmul(bank(0)[:, g * P:(g + 1) * P], qb[:, g, :], hstate[:, g, :], start=True, stop=True)
                    for hh in range(2):
                        h = 2 * g + hh
                        mm = e.matmul(bank(0)[:, h * 64:(h + 1) * 64], sc[:, 2 * hh + g, :], pin[:, I_AT + h * 64:I_AT + (h + 1) * 64],
                                      start=False, stop=True, skip_group_check=True)
                mm.then_inc(sems["ho_done"], 1)
                e.wait_ge(sems["r"], BASE + t + 1)
                e.wait_ge(sems["tt"], BASE + NX * t + NX)
                for h in range(DNH):
                    mm = e.matmul(bank(5)[:, h * P:(h + 1) * P], tb[:, 1, h, :], kb[:, h, :], start=True, stop=True)
                mm.then_inc(sems["vn_done"], 1)
                e.wait_ge(sems["kdt"], BASE + t + 1)
                e.wait_ge(sems["xy"], BASE + NX * t + NX)
                for g in range(2):
                    mm = e.matmul(bank(2)[:, g * P:(g + 1) * P], kdt[:, g, :], pin[:, I_AT + g * P:I_AT + (g + 1) * P],
                                  start=True, stop=True)
                mm.then_inc(sems["hs_done"], 1)
                e.wait_ge(sems["vn"], BASE + t + 1)
                e.wait_ge(sems["at"], BASE + t + 1)
                for h in range(DNH):
                    e.matmul(bank(6)[:, h * P:(h + 1) * P], qdt[:, h, :], state[:, h, :], start=True, stop=False)
                    mm = e.matmul(bank(6)[:, h * P:(h + 1) * P], at[:, h, :], qd[:, h, :], start=False, stop=True)
                mm.then_inc(sems["o_done"], 1)
                e.wait_ge(sems["kd"], BASE + t + 1)
                for h in range(DNH):
                    mm = e.matmul(bank(7)[:, h * P:(h + 1) * P], kd[:, h, :], qd[:, h, :], start=True, stop=True)
                mm.then_inc(sems["su_done"], 1)
                e.wait_ge(sems["fin"], BASE + t + 1)
                for n in range(2):
                    for k in range(4):
                        c = (4 * n + k) * P
                        mm = e.transpose(bank(3 + n)[:, k * P:(k + 1) * P], mix[:, c:c + P], ident[:, :])
                    mm.then_inc(sems["mt_done"], 1)

        def mixer_act(e):
            with e.Fori(0, NT) as t:
                def act(dst, src, func, name, **kw):
                    e.activation(dst, src, func, **kw).then_inc(sems[name], 1)

                e.wait_ge(sems["pin_loaded"], BASE + 16 * t + 16)
                e.wait_ge(sems["m_sums"], BASE + 3 * t - 2)
                act(sq[:, :], pin[:, 0:2 * DNW], ACT.Square, "sq")
                e.wait_ge(sems["h_abs"], BASE + t + 1)
                act(hls[:, :, :], hls[:, :, :], ACT.Exp, "h_exp", scale=-1.0)
                e.wait_ge(sems["h_exp"], BASE + t + 1)
                act(hls[:, :, :], hls[:, :, :], ACT.Ln, "h_ln", bias=1.0)
                e.wait_ge(sems["dn_ssq"], BASE + t + 1)
                act(r8[:, :], r8[:, :], ACT.Ln, "dn_ln", bias=eps_col[:, 0:1])
                e.wait_ge(sems["dn_ln"], BASE + t + 1)
                act(r8[:, :], r8[:, :], ACT.Exp, "dn_r", scale=-0.5)
                e.wait_ge(sems["zg_abs"], BASE + t + 1)
                act(gate[:, SBW:], gate[:, SBW:], ACT.Exp, "zg_exp", scale=-1.0)
                e.wait_ge(sems["zg_exp"], BASE + t + 1)
                act(gate[:, SBW:], gate[:, SBW:], ACT.Ln, "zg_ln", bias=1.0)
                e.wait_ge(sems["h_ls"], BASE + t + 1)
                e.wait_ge(sems["h_qe"], BASE + 2 * t)
                e.wait_ge(sems["h_qb"], BASE + t)
                e.wait_ge(sems["h_ke"], BASE + 2 * t)
                e.wait_ge(sems["h_kd"], BASE + t)
                act(hq[:, :, :], hls[:, 0:2, :], ACT.Exp, "h_sq")
                e.wait_ge(sems["h_k0"], BASE + t + 1)
                act(hk[:, :, :], hk[:, :, :], ACT.Exp, "h_k")
                for n, (dst, name) in enumerate(((kt, "m"), (kbt, "m"), (qt, "m"), (qdt, "o_done"))):
                    e.wait_ge(sems["turned"], BASE + 4 * t + n + 1)
                    if n == 0:
                        e.wait_ge(sems["ks_done"], BASE + t)
                    if n == 1:
                        e.wait_ge(sems["kk_done"], BASE + 3 * t)
                    if n == 3:
                        e.wait_ge(sems["o_done"], BASE + t)
                    act(dst[:, :, :], heads(bank(n)), ACT.Copy, "turned_copy")
                    if n == 1:
                        e.wait_ge(sems["a_min"], BASE + t + 1)
                        act(dtr[:, :, :], dtr[:, :, :], ACT.Exp, "dt")
                        e.wait_ge(sems["a_max"], BASE + t + 1)
                        act(span[:, :, :], span[:, :, :], ACT.Exp, "dd", scale=-1.0)
                e.wait_ge(sems["h_b"], BASE + 2 * t + 2)
                e.wait_ge(sems["hs_dec"], BASE + t)
                act(eb[:, :, :], hb[:, :, :], ACT.Exp, "h_eb")
                e.wait_ge(sems["h_kd0"], BASE + t + 1)
                act(kdc[:, :, :], kdc[:, :, :], ACT.Exp, "h_kd1")
                for q in range(2):
                    e.wait_ge(sems["h_dabs"], BASE + 2 * t + q + 1)
                    act(el[:, :, :, :], el[:, :, :, :], ACT.Exp, "h_el", scale=-1.0)
                    if q == 0:
                        e.wait_ge(sems["zg_ls"], BASE + t + 1)
                        act(gate[:, SBW:], gate[:, SBW:], ACT.Exp, "zg_sg")
                e.wait_ge(sems["kdt_done"], BASE + t + 1)
                act(kdt[:, :, :], bank(1)[:, 0:2 * P].rearrange("p (g c) -> p g c", c=P), ACT.Copy, "kdt")
                e.wait_ge(sems["ho_done"], BASE + t + 1)
                e.wait_ge(sems["mt_done"], BASE + 2 * t)
                act(mix[:, SBW + DNW:], bank(0)[:, 0:HGW], ACT.Copy, "mix_hg")
                e.wait_ge(sems["vn_done"], BASE + t + 1)
                act(qd[:, :, :], heads(bank(5)), ACT.Copy, "vn")
                e.wait_ge(sems["o_done"], BASE + t + 1)
                act(mix[:, SBW:SBW + DNW], bank(6), ACT.Copy, "mix_dn")
                e.wait_ge(sems["mix_dn"], BASE + t + 1)
                e.wait_ge(sems["mix_sb"], BASE + t + 1)
                act(sq[:, :], mix[:, :], ACT.Square, "msq")
                e.wait_ge(sems["m_sums"], BASE + 3 * t + 3)
                act(r16[:, :], r16[:, :], ACT.Ln, "m_ln", scale=1.0 / 64, bias=eps_col[:, 0:1])
                e.wait_ge(sems["m_ln"], BASE + t + 1)
                act(r16[:, :], r16[:, :], ACT.Exp, "m_r", scale=-0.5)
                for n in range(2):
                    e.wait_ge(sems["mt_done"], BASE + 2 * t + n + 1)
                    act(act_h[:, 4 * n:4 * n + 4, ds(t * P, P)], heads(bank(3 + n)), ACT.Copy, "act_high")

        def mixer_pool(e):
            mixed_to_dram(e)
            for v in (sc[:, :, :], state[:, :, :], hstate[:, :, :]):
                e.memset(v, 0.0).then_inc(sems["zeroed"], 1)
            e.wait_ge(sems["gains_loaded"], BASE + 16 * (SBH + DNH + 4))
            e.tensor_copy(gate[:, 0:SBW], gain_row[:, 0:SBW]).then_inc(sems["zeroed"], 1)
            e.wait_ge(sems["decay_act"], BASE + 7)
            e.wait_ge(sems["decay_dve"], BASE + 9)
            with e.Fori(0, NT) as t:
                def mul(dst, x, y, name):
                    e.tensor_tensor(dst, x, y, ALU.mult).then_inc(sems[name], 1)

                e.wait_ge(sems["m"], BASE + t)
                mul(span[:, :, :], upto[:, :].unsqueeze(1).to_broadcast([P, DNH, P]), per_head(g_all, t), "gup")
                e.wait_ge(sems["vn_done"], BASE + t)
                mul(tb[:, :, :, :].rearrange("p z h c -> p (z h) c"), ident[:, :].unsqueeze(1).to_broadcast([P, 2 * DNH, P]),
                    ones[:, :].unsqueeze(1).to_broadcast([P, 2 * DNH, P]), "t_init")
                e.wait_ge(sems["pin_loaded"], BASE + 16 * t + 16)
                mul(vv, vv, per_head(beta, t), "vb")
                e.wait_ge(sems["qkn"], BASE + t + 1)
                e.wait_ge(sems["su_done"], BASE + t)
                mul(kd[:, :, :], kn, per_head(rest, t), "kd")
                e.wait_ge(sems["h_q"], BASE + t + 1)
                e.wait_ge(sems["h_eb"], BASE + t + 1)
                e.wait_ge(sems["ho_done"], BASE + t)
                mul(qb[:, :, :], hq[:, :, :], eb[:, :, :], "h_qb")
                e.wait_ge(sems["h_kd1"], BASE + t + 1)
                e.wait_ge(sems["h_k"], BASE + t + 1)
                mul(kdc[:, :, :], kdc[:, :, :], hk[:, :, :], "h_kd")
                e.wait_ge(sems["at0"], BASE + t + 1)
                mul(at[:, :, :], at[:, :, :], upto[:, :].unsqueeze(1).to_broadcast([P, DNH, P]), "at")
                for q in range(2):
                    e.wait_ge(sems["h_el"], BASE + 2 * t + q + 1)
                    e.wait_ge(sems["h_p"], BASE + 8 * t + 4 * q)
                    mul(ke[:, :, :, :], el[:, :, :, :], hk[:, :, :].unsqueeze(1).to_broadcast([P, 4, 2, P]), "h_ke")
                    if q == 0:
                        e.wait_ge(sems["zg_sg"], BASE + t + 1)
                        mul(gate[:, SBW:SBW + DNW], gate[:, SBW:SBW + DNW], pin[:, Z_AT:Z_AT + DNW], "gated")
                        e.wait_ge(sems["gated"], BASE + 2 * t + 1)
                        mul(gate[:, SBW:], gate[:, SBW:], gain_row[:, SBW:], "gated")
                        e.wait_ge(sems["mt_done"], BASE + 2 * t)
                        mul(mix[:, 0:SBW].rearrange("p (h c) -> p h c", c=P), pin[:, SB_AT:].rearrange("p (h c) -> p h c", c=P),
                            ones[:, :].unsqueeze(1).to_broadcast([P, SBW // P, P]), "mix_sb")
                e.wait_ge(sems["ho_done"], BASE + t + 1)
                mul(hstate[:, :, :], hstate[:, :, :], eb[:, :, P - 1:P].to_broadcast([P, 2, P]), "hs_dec")
                e.wait_ge(sems["o_done"], BASE + t + 1)
                mul(state[:, :, :], state[:, :, :], per_head(whole, t), "s_dec")
                e.wait_ge(sems["m_n"], BASE + t + 1)
                e.wait_ge(sems["gated"], BASE + 2 * t + 2)
                mul(mix[:, :], mix[:, :], gate[:, :], "fin")

        def mixer_dve(e):
            e.wait_ge(sems["zeroed"], BASE + 4)
            with e.Fori(0, NT) as t:
                def tt(dst, x, y, op, name):
                    e.tensor_tensor(dst, x, y, op).then_inc(sems[name], 1)

                def ts(dst, x, v, op, name):
                    e.tensor_scalar(dst, x, v, None, op).then_inc(sems[name], 1)

                e.wait_ge(sems["cin_loaded"], BASE + 16 * t + 16)
                absolute_value(e, hls[:, :, :], cin[:, :, :]).then_inc(sems["h_abs"], 1)
                e.wait_ge(sems["sq"], BASE + t + 1)
                e.reduce_sum(r8[:, :], sq[:, :].rearrange("p (h c) -> p h c", c=P), AX.X).then_inc(sems["dn_ssq"], 1)
                e.wait_ge(sems["fin"], BASE + t)
                absolute_value(e, gate[:, SBW:], pin[:, Z_AT:Z_AT + DNW + HGW]).then_inc(sems["zg_abs"], 1)
                e.wait_ge(sems["h_ln"], BASE + t + 1)
                e.scalar_tensor_tensor(out=hls[:, :, :], in0=cin[:, :, :], scalar=0.0, in1=hls[:, :, :],
                                            op0=ALU.min, op1=ALU.subtract).then_inc(sems["h_ls"], 1)
                e.wait_ge(sems["dn_r"], BASE + t + 1)
                ts(r8[:, 0:DNH], r8[:, 0:DNH], float(P) ** -0.5, ALU.mult, "dn_rq")
                e.wait_ge(sems["h_ls"], BASE + t + 1)
                e.wait_ge(sems["h_ke"], BASE + 2 * t)
                e.wait_ge(sems["h_kd"], BASE + t)
                tt(hk[:, :, :], hls[:, 2:4, :], cin[:, 2:4, :], ALU.subtract, "h_k0")
                e.wait_ge(sems["dn_rq"], BASE + t + 1)
                tt(qk, qk, r8[:, :].unsqueeze(2).to_broadcast([P, 2 * DNH, P]), ALU.mult, "qkn")
                e.wait_ge(sems["qkn"], BASE + t + 1)
                e.wait_ge(sems["vn_done"], BASE + t)
                tt(kb[:, :, :], kn, per_head(beta, t), ALU.mult, "kb")
                e.wait_ge(sems["su_done"], BASE + t)
                tt(qd[:, :, :], qn, per_head(eg, t), ALU.mult, "qd")
                e.wait_ge(sems["gr_done"], BASE + t + 1)
                tt(span[:, :, :], heads(bank(7)), per_head(gc, t), ALU.subtract, "a1")
                e.wait_ge(sems["a1"], BASE + t + 1)
                ts(dtr[:, :, :], span[:, :, :], 0.0, ALU.min, "a_min")
                ts(span[:, :, :], span[:, :, :], 0.0, ALU.max, "a_max")
                e.wait_ge(sems["h_sq"], BASE + t + 1)
                tt(hq[:, :, :], hq[:, :, :], cin[:, 0:2, :], ALU.mult, "h_q")
                e.wait_ge(sems["h_eb"], BASE + t)
                for g in range(2):
                    e.tensor_tensor_scan(hb[:, g, :], ones[:, :], hls[:, 2 + g, :], 0.0, ALU.mult, ALU.add).then_inc(sems["h_b"], 1)
                e.wait_ge(sems["h_b"], BASE + 2 * t + 2)
                e.wait_ge(sems["kdt_done"], BASE + t)
                tt(kdc[:, :, :], hb[:, :, P - 1:P].to_broadcast([P, 2, P]), hb[:, :, :], ALU.subtract, "h_kd0")
                e.wait_ge(sems["zg_ln"], BASE + t + 1)
                e.scalar_tensor_tensor(out=gate[:, SBW:], in0=pin[:, Z_AT:Z_AT + DNW + HGW], scalar=0.0, in1=gate[:, SBW:],
                                            op0=ALU.min, op1=ALU.subtract).then_inc(sems["zg_ls"], 1)

                def spread(q):
                    e.wait_ge(sems["h_ke"], BASE + 2 * t + q)
                    for n in range(4):
                        lv = 4 * q + n
                        if lv == LEVELS:
                            tt(el[:, n, :, :], hb[:, :, :], hb[:, :, :], ALU.subtract, "h_dl")
                            continue
                        h = P >> (lv + 1)
                        v = hb[:, :, :].rearrange("p g (b r) -> p (g b) r", r=2 * h)
                        tt(el[:, n, :, :].rearrange("p g (b r) -> p (g b) r", r=2 * h), v,
                           v[:, :, h - 1:h].to_broadcast([P, P // h, 2 * h]), ALU.subtract, "h_dl")
                    e.wait_ge(sems["h_dl"], BASE + 8 * t + 4 * q + 4)
                    absolute_value(e, el[:, :, :, :], el[:, :, :, :]).then_inc(sems["h_dabs"], 1)

                def queries(q):
                    e.wait_ge(sems["h_el"], BASE + 2 * t + q + 1)
                    e.wait_ge(sems["h_p"], BASE + 8 * t + 4 * q)
                    e.wait_ge(sems["h_q"], BASE + t + 1)
                    tt(qe[:, :, :, :], el[:, :, :, :], hq[:, :, :].unsqueeze(1).to_broadcast([P, 4, 2, P]), ALU.mult, "h_qe")

                def take_scores(lv):
                    e.wait_ge(sems["h_p"], BASE + 8 * t + lv + 1)
                    e.wait_ge(sems["h_sc"], BASE + 8 * t + lv)
                    if lv == 0:
                        e.wait_ge(sems["ho_done"], BASE + t)
                    hold(e, lv)
                    e.copy_predicated(sc[:, :, :].rearrange("p (z g) c -> p z g c", g=2),
                                           pair_mask[:, lv, :].bitcast(I32).unsqueeze(1).unsqueeze(1).to_broadcast([P, 2, 2, P]),
                                           banks[3 * (lv % 2)][:, :, 0:2 * P].rearrange("p z (g c) -> p z g c", c=P)).then_inc(sems["h_sc"], 1)

                def pack(lv):
                    s = 2 ** lv
                    if lv == 0:
                        e.wait_ge(sems["mt"], BASE + t + 1)
                        e.wait_ge(sems["d_done"], BASE + 6 * t)
                        src = [v[:, :, :].rearrange("p h (b z) -> p h b z", z=2)[:, :, :, z] for z, v in enumerate((mm_, mt))]
                    else:
                        e.wait_ge(sems["x_done"], BASE + 6 * t + lv)
                        v = bank(2).rearrange("p (z h c) -> p z h c", h=DNH, c=64)
                        src = [v[:, z] for z in range(2)]
                    for z, m in enumerate((row_mask, col_mask)):
                        if not (z == 0 and lv == LEVELS - 1):
                            tt(xy[:, z], src[z], mask_of(m, lv), ALU.mult, "xy")

                def update(lv):
                    s = 2 ** lv
                    if lv == 0:
                        e.wait_ge(sems["xy"], BASE + NX * t + 2)
                        e.wait_ge(sems["t_init"], BASE + t + 1)
                        new = [xy[:, z] for z in range(2)]
                    else:
                        e.wait_ge(sems["d_done"], BASE + 6 * t + lv)
                        v = bank(3).rearrange("p (z h c) -> p z h c", h=DNH, c=64)
                        new = [v[:, z] for z in range(2)]
                    for z, part in enumerate((left, right)):
                        if z == 0 and lv == LEVELS - 1:
                            continue
                        dst = part(tb[:, z, :, :], s)
                        tt(dst, dst, blocks(new[z], s), ALU.subtract, "tt")

                spread(0)
                e.wait_ge(sems["kk_done"], BASE + 3 * t + 1)
                e.wait_ge(sems["dd"], BASE + t + 1)
                tt(mm_[:, :, :], heads(bank(4)), span[:, :, :], ALU.mult, "m")
                e.wait_ge(sems["kk_done"], BASE + 3 * t + 2)
                e.wait_ge(sems["dt"], BASE + t + 1)
                tt(mt[:, :, :], heads(bank(5)), dtr[:, :, :], ALU.mult, "mt")
                e.wait_ge(sems["kk_done"], BASE + 3 * t + 3)
                tt(at[:, :, :], heads(bank(6)), dtr[:, :, :], ALU.mult, "at0")
                pack(0); update(0)
                queries(0)
                pack(1); take_scores(0); update(1); take_scores(1)
                pack(2); take_scores(2); update(2); take_scores(3)
                spread(1)
                e.wait_ge(sems["ks_done"], BASE + t + 1)
                e.wait_ge(sems["turned"], BASE + 4 * t + 2)
                tt(kb[:, :, :], heads(bank(4)), per_head(neg_be, t), ALU.mult, "ks")
                pack(3); update(3)
                queries(1)
                e.wait_ge(sems["ks"], BASE + t + 1)
                e.wait_ge(sems["vb"], BASE + t + 1)
                tt(kb[:, :, :], kb[:, :, :], vv, ALU.add, "r")
                pack(4); take_scores(4); update(4); take_scores(5)
                pack(5); take_scores(6); update(5); take_scores(7)
                pack(6); update(6)
                e.wait_ge(sems["hs_done"], BASE + t + 1)
                tt(htmp[:, :, :], bank(2)[:, 0:2 * P].rearrange("p (g c) -> p g c", c=P),
                   head_mask[:, :].unsqueeze(1).to_broadcast([P, 2, P]), ALU.mult, "htmp")
                e.wait_ge(sems["htmp"], BASE + t + 1)
                e.wait_ge(sems["hs_dec"], BASE + t + 1)
                tt(hstate[:, :, :], hstate[:, :, :], htmp[:, :, :], ALU.add, "hs_new")
                e.wait_ge(sems["su_done"], BASE + t + 1)
                e.wait_ge(sems["s_dec"], BASE + t + 1)
                tt(state[:, :, :], state[:, :, :], heads(bank(7)), ALU.add, "s_new")
                e.wait_ge(sems["msq"], BASE + t + 1)
                e.reduce_sum(r16[:, :], sq[:, :].rearrange("p (h c) -> p h c", c=64), AX.X).then_inc(sems["m_sums"], 1)
                e.wait_ge(sems["m_sums"], BASE + 3 * t + 1)
                pairs = r16[:, 4:4 + 2 * DNH].rearrange("p (h z) -> p h z", z=2)
                e.reduce_sum(r4[:, :], pairs, AX.X).then_inc(sems["m_sums"], 1)
                e.wait_ge(sems["m_sums"], BASE + 3 * t + 2)
                ts(pairs, r4[:, :].unsqueeze(2).to_broadcast([P, DNH, 2]), 0.5, ALU.mult, "m_sums")
                e.wait_ge(sems["m_r"], BASE + t + 1)
                tt(mix[:, :].rearrange("p (h c) -> p h c", c=64), mix[:, :].rearrange("p (h c) -> p h c", c=64),
                   r16[:, :].unsqueeze(2).to_broadcast([P, 16, 64]), ALU.mult, "m_n")
                for n in range(2):
                    e.wait_ge(sems["act_high"], BASE + 2 * t + n + 1)
                    tt(act_l[:, 4 * n:4 * n + 4, ds(t * P, P)], heads(bank(3 + n)),
                       act_h[:, 4 * n:4 * n + 4, ds(t * P, P)].bitcast(F32), ALU.subtract, "act_low")

        def out_sync(e):
            load_tile(e, W_OUT + 1, (W_OUT + 1) % 2, w_out[:, :, P:2 * P])
            with e.Fori(1, KT // 2) as i:
                for b in range(2):
                    w = W_OUT + 2 * i + b
                    load_tile(e, w, (W_OUT + b) % 2, w_out[:, :, ds((2 * i + b) * P, P)])

        def out_pe(e):
            e.wait_ge(sems["act_low"], BASE + 2 * NT)
            with e.Fori(0, KT // 2) as i:
                for b in range(2):
                    n = 2 * i + b
                    for th in range(2):
                        dense_half(e, W_OUT + n, (W_OUT + b) % 2, th, bank(th))
                    for th in range(2):
                        e.wait_ge(sems["dense_evac"], BASE + 2 * (W_OUT + n) + th + 1)
                        e.wait_ge(sems["x1_ready"], BASE + 2 * n + th - 1)
                        for j in range(4):
                            c = th * HALF + j * P
                            mm = e.transpose(bank(2 + th)[:, j * P:(j + 1) * P], x_t[:, b, c:c + P], ident[:, :])
                        mm.then_inc(sems["x_turned"], 1)

        def out_act(e):
            with e.Fori(0, KT // 2) as i:
                for b in range(2):
                    w = W_OUT + 2 * i + b
                    split_high(e, w + 1, (W_OUT + b + 1) % 2)
                    for th in range(2):
                        e.wait_ge(sems["dense_done"], BASE + 2 * w + th + 1)
                        e.wait_ge(sems["x_turned"], BASE + 4 * i + 2 * b - 2)
                        e.activation(x_t[:, b, th * HALF:(th + 1) * HALF], bank(th), ACT.Copy).then_inc(sems["dense_evac"], 1)

        def out_pool(e):
            with e.Fori(0, KT // 2) as i:
                for b in range(2):
                    split_low(e, W_OUT + 2 * i + b + 1, (W_OUT + b + 1) % 2)

        def out_dve(e):
            for n in range(NT // 2):
                e.wait_ge(sems[f"x_loaded{n}"], BASE + 32)
            with e.Fori(0, KT // 2) as i:
                for b in range(2):
                    for th in range(2):
                        n = 4 * i + 2 * b + th
                        e.wait_ge(sems["x_turned"], BASE + n + 1)
                        dst = x_sb[:, 4 * th:4 * th + 4, ds((2 * i + b) * P, P)]
                        e.tensor_tensor(dst, dst, heads(bank(2 + th)), ALU.add).then_inc(sems["x1_ready"], 1)

        W_F1 = W_FF + 2

        def ff_loop(e, step):
            step(0, W_FF, W_FF % 2, 0, True, False)
            with e.Fori(0, (NF - 2) // 2) as i:
                for r in range(2):
                    step(2 * i + 1 + r, W_F1 + 6 * i + 3 * r, (W_F1 + 3 * r) % 2, (1 + r) % 2, False, False)
            step(NF - 1, W_F1 + 3 * (NF - 2), (W_F1 + 3 * (NF - 2)) % 2, (NF - 1) % 2, False, False)
            step(NF, W_F1 + 3 * (NF - 1) - 2, (W_F1 + 3 * (NF - 1)) % 2, NF % 2, False, True)

        def ff_sync(e):
            def step(f, w, b, fp, first, last):
                if not last and not first:
                    load_tile(e, w, b, w_gate[:, :, ds(f * P, P)])
                    load_tile(e, w + 1, 1 - b, w_up[:, :, ds(f * P, P)])
                if not first:
                    load_tile(e, w + 2, b, w_down[:, f - 1, :].rearrange("p (k c) -> p k c", c=P))
            ff_loop(e, step)

        def ff_pe(e):
            e.wait_ge(sems["norm_l"], BASE + 2 * NT)

            def product(w, b, th, dst):
                e.wait_ge(sems["wl_ready"], BASE + w + 1)
                cols = slice(th * HALF, (th + 1) * HALF)
                for k in range(KT):
                    e.matmul(dst, w_h[:, b, k], act_h[:, k, cols], start=(k == 0), stop=False)
                    e.matmul(dst, w_h[:, b, k], act_l[:, k, cols], start=False, stop=False)
                    mm = e.matmul(dst, w_l[:, b, k], act_h[:, k, cols], start=False, stop=(k == KT - 1))
                mm.then_inc(sems["gu_done"], 1)

            def step(f, w, b, fp, first, last):
                if not last:
                    for th in range(2):
                        e.wait_ge(sems["ff_silu"], BASE + 2 * f + th - 1)
                        product(w, b, th, bank(th))
                    for th in range(2):
                        e.wait_ge(sems["ff_mul"], BASE + 2 * f + th - 1)
                        product(w + 1, 1 - b, th, bank(2 + th))
                if not first:
                    e.wait_ge(sems["wl_ready"], BASE + w + 3)
                    e.wait_ge(sems["ff_low"], BASE + 2 * f)
                    for c in range(2 * NT):
                        t, n = c // 2, c % 2
                        e.wait_ge(sems["x_added"], BASE + 16 * (f - 1) + c - 3)
                        rows = slice(t * P, (t + 1) * P)
                        dst = bank(4 + c % 4)
                        e.matmul(dst, ff_h[:, 1 - fp, rows], w_h[:, b, 4 * n:4 * n + 4, :], start=True, stop=False)
                        e.matmul(dst, ff_h[:, 1 - fp, rows], w_l[:, b, 4 * n:4 * n + 4, :], start=False, stop=False)
                        e.matmul(dst, ff_l[:, 1 - fp, rows], w_h[:, b, 4 * n:4 * n + 4, :], start=False, stop=True).then_inc(sems["down_done"], 1)
            ff_loop(e, step)

        def ff_act(e):
            def high(w, b, name, count):
                e.wait_ge(sems[f"w_loaded{b}"], BASE + 8 * (w - b) + 16)
                e.wait_ge(sems[name], BASE + count)
                e.activation(w_h[:, b], w_raw[:, b], ACT.Copy).then_inc(sems["wh_ready"], 1)

            def step(f, w, b, fp, first, last):
                if last:
                    return
                if first:
                    high(w + 1, 1 - b, "dense_done", 2 * W_FF)
                else:
                    high(w + 1, 1 - b, "down_done", 16 * (f - 1))
                for th in range(2):
                    e.wait_ge(sems["gu_done"], BASE + 4 * f + th + 1)
                    e.wait_ge(sems["ff_mul"], BASE + 2 * f + th - 1)
                    e.activation(gs[:, th, :], bank(th), ACT.Silu).then_inc(sems["ff_silu"], 1)
                if not first:
                    high(w + 2, b, "gu_done", 4 * f + 2)
                for th in range(2):
                    e.wait_ge(sems["ff_mul"], BASE + 2 * f + th + 1)
                    if not first:
                        e.wait_ge(sems["down_done"], BASE + 16 * (f - 1))
                    e.activation(ff_h[:, fp, th * HALF:(th + 1) * HALF], ffv[:, th, :], ACT.Copy).then_inc(sems["ff_high"], 1)
                if first:
                    high(w + 2, b, "gu_done", 2)
                else:
                    high(w + 3, 1 - b, "gu_done", 4 * f + 4)
            ff_loop(e, step)

        def ff_pool(e):
            def step(f, w, b, fp, first, last):
                if last:
                    return
                split_low(e, w + 1, 1 - b)
                if not first:
                    split_low(e, w + 2, b)
                for th in range(2):
                    e.wait_ge(sems["ff_high"], BASE + 2 * f + th + 1)
                    cols = slice(th * HALF, (th + 1) * HALF)
                    e.tensor_tensor(ff_l[:, fp, cols], ffv[:, th, :], ff_h[:, fp, cols].bitcast(F32), ALU.subtract).then_inc(sems["ff_low"], 1)
                if first:
                    split_low(e, w + 2, b)
                else:
                    split_low(e, w + 3, 1 - b)
            ff_loop(e, step)

        def ff_dve(e):
            def step(f, w, b, fp, first, last):
                if not last:
                    for th in range(2):
                        e.wait_ge(sems["gu_done"], BASE + 4 * f + th + 3)
                        e.wait_ge(sems["ff_silu"], BASE + 2 * f + th + 1)
                        e.wait_ge(sems["ff_low"], BASE + 2 * f + th - 1)
                        e.tensor_tensor(ffv[:, th, :], bank(2 + th), gs[:, th, :], ALU.mult).then_inc(sems["ff_mul"], 1)
                if not first:
                    for c in range(2 * NT):
                        t, n = c // 2, c % 2
                        e.wait_ge(sems["down_done"], BASE + 16 * (f - 1) + c + 1)
                        dst = x_sb[:, t, n * HALF:(n + 1) * HALF]
                        e.tensor_tensor(dst, dst, bank(4 + c % 4), ALU.add).then_inc(sems["x_added"], 1)
            ff_loop(e, step)

        def last_act(e):
            for t in range(NT):
                e.wait_ge(sems["x_added"], BASE + 16 * (NF - 1) + 2 * t + 2)
                e.wait_ge(sems["norm_ssq"], BASE + 2 * NT + t)
                e.activation(junk, x_sb[:, t, :], ACT.Square, accum_out=ssq[:, t:t + 1]).then_inc(sems["norm_ssq"], 1)
            e.wait_ge(sems["norm_ssq"], BASE + 3 * NT)
            e.activation(lnv[:, :], ssq[:, :], ACT.Ln, scale=1.0 / D, bias=eps_col[:, 0:1]).then_inc(sems["norm_ln"], 1)
            e.wait_ge(sems["norm_ln"], BASE + 2 * NT + 1)
            e.activation(rstd[:, :], lnv[:, :], ACT.Exp, scale=-0.5).then_inc(sems["norm_rstd"], 1)

        def last_dve(e):
            e.wait_ge(sems["norm_rstd"], BASE + 2 * NT + 1)
            e.wait_ge(sems["gain_loaded"], BASE + 48)
            for t in range(NT):
                e.scalar_tensor_tensor(out=x_sb[:, t, :], in0=x_sb[:, t, :], scalar=rstd[:, t:t + 1], in1=gain_row[:, :],
                                            op0=ALU.mult, op1=ALU.mult).then_inc(sems["out_ready"], 1)

        def last_sync(e):
            for t in range(NT):
                e.wait_ge(sems["out_ready"], BASE + t + 1)
                e.dma_start(out_rows[:, t, :], x_sb[:, t, :]).then_inc(sems["out_stored"], 16)
            e.wait_ge(sems["out_stored"], BASE + 16 * NT)

        CONSTS = 13 + 5 + 2 * 6 + 2 * LEVELS + 3 * LEVELS + 1 + 2

        @block.sync
        def _(e):
            e.wait_ge(sems["consts"], 1)
            for n in range(NT // 2):
                e.dma_start(x_sb[:, 2 * n:2 * n + 2, :], x_rows[:, 2 * n:2 * n + 2, :]).then_inc(sems[f"x_loaded{n}"], 16)
            e.dma_start(gain_row[:, :], a["norm1"][0].partition_broadcast(P)).then_inc(sems["gain_loaded"], 16)
            e.dma_start(cw_rows[0:4 * NC, :], a["dn_conv"][0].rearrange("k (c p) -> (k c) p", p=P)).then_inc(sems["small_loaded"], 16)
            e.dma_start(dt_row[:, :], a["dn_dt_bias"][0].partition_broadcast(P)).then_inc(sems["rows_loaded"], 16)
            e.dma_start(rate_log[:, :], a["dn_a_log"][0].partition_broadcast(P)).then_inc(sems["rows_loaded"], 16)
            first_sync(e)
            e.wait_ge(sems["norm_xn"], BASE + NT)
            for first, n, width, name in ((0, SBH, SBD, "sb_gain"), (SBW, DNH, P, "dn_gain"), (SBW + DNW, 4, HGD, "hg_gain")):
                for h in range(n):
                    at = first + h * width
                    e.dma_start(gain_row[:, at:at + width], a[name][0].partition_broadcast(P)).then_inc(sems["gains_loaded"], 16)
            lead_sync(e)
            load_tile(e, W_OUT, W_OUT % 2, w_out[:, :, 0:P])
            mixed_to_dram(e)
            mixer_sync(e)
            e.wait_ge(sems["act_low"], BASE + 2 * NT)
            e.wait_ge(sems["fin"], BASE + NT)
            e.dma_start(gain_row[:, :], a["norm2"][0].partition_broadcast(P)).then_inc(sems["gain_loaded"], 16)
            for n in range(NT // 2):
                e.dma_start(x_sb[:, 2 * n:2 * n + 2, :], x_rows[:, 2 * n:2 * n + 2, :]).then_inc(sems[f"x_loaded{n}"], 16)
            out_sync(e)
            load_tile(e, W_FF, W_FF % 2, w_gate[:, :, 0:P])
            load_tile(e, W_FF + 1, (W_FF + 1) % 2, w_up[:, :, 0:P])
            e.wait_ge(sems["norm_xn"], BASE + 2 * NT)
            e.dma_start(gain_row[:, :], a["final_norm"].partition_broadcast(P)).then_inc(sems["gain_loaded"], 16)
            ff_sync(e)
            last_sync(e)

        @block.gpsimd
        def _(e):
            assert masks(e) == CONSTS
            first_pool(e)
            mix_pool(e)
            mixer_pool(e)
            out_pool(e)
            ff_pool(e)

        @block.scalar
        def _(e):
            e.preload_act_table_set("natural_log_exp_and_others")
            e.wait_ge(sems["consts"], CONSTS)
            norm_act(e, 0)
            first_act(e)
            mix_act(e)
            decay_act(e)
            mixer_act(e)
            out_act(e)
            norm_act(e, 1)
            ff_act(e)
            last_act(e)

        @block.vector
        def _(e):
            e.wait_ge(sems["consts"], CONSTS)
            norm_dve(e, 0)
            first_dve(e)
            mix_dve(e)
            decay_dve(e)
            mixer_dve(e)
            out_dve(e)
            norm_dve(e, 1)
            ff_dve(e)
            last_dve(e)

        @block.tensor
        def _(e):
            e.wait_ge(sems["consts"], CONSTS)
            norm_pe(e, 0)
            e.wait_ge(sems["norm_l"], BASE + NT)
            first_pe(e)
            mix_pe(e)
            decay_pe(e)
            mixer_pe(e)
            out_pe(e)
            norm_pe(e, 1)
            ff_pe(e)


INPUTS = ("x", "norm1", "w_in", "sb_gain", "dn_conv", "dn_a_log", "dn_dt_bias", "dn_gain", "hg_lb_logits", "hg_gain",
          "w_out", "norm2", "w_gate", "w_up", "w_down", "final_norm")


def kernel(**inputs):
    import numpy as np
    import concourse.bacc as bacc
    from concourse.bass_utils import run_bass_kernel_spmd

    nc = bacc.Bacc("TRN2", target_bir_lowering=False, num_devices=1)
    arrays, args = {}, {}
    for name in INPUTS:
        arrays[f"in_{name}"] = np.ascontiguousarray(inputs[name])
        args[name] = nc.dram_tensor(f"in_{name}", arrays[f"in_{name}"].shape, F32, kind="ExternalInput").ap()
    out = nc.dram_tensor("out", inputs["x"].shape, F32, kind="ExternalOutput").ap()
    trunk_program(nc, args, out)
    got = run_bass_kernel_spmd(nc, [arrays], core_ids=[0])
    return got.results[0]["out"]
```

```python
import concourse.bass as bass
from concourse import mybir
from contextlib import ExitStack

F32 = mybir.dt.float32
F32R = mybir.dt.float32r
I32 = mybir.dt.int32
ALU = mybir.AluOpType
ACT = mybir.ActivationFunctionType
AX = mybir.AxisListType
ds = bass.ds

P = 128
HALF = 512
EPS = 1e-6
BASE = 3
LEVELS = 7


def trunk_program(nc, a, out):
    T, D = a["x"].shape[1:]
    F = a["w_gate"].shape[2]
    NT, KT, NF = T // P, D // P, F // P
    SBH = 4
    SBD = a["sb_gain"].shape[1]
    DNH = a["dn_a_log"].shape[1]
    HGD = a["hg_gain"].shape[1]
    SBW, DNW, HGW = SBH * SBD, DNH * P, D // 4
    NC = 3 * DNW // P
    C_DN = 3 * SBW
    C_Z = C_DN + 3 * DNW
    C_AB = C_Z + DNW
    C_HQ = C_AB + 2 * DNH
    C_HF, C_HI, C_HG = C_HQ + HGW, C_HQ + 2 * HGW, C_HQ + 3 * HGW
    def tile_of(kind, j, first, per_pass, at):
        return kind, first + j * P, per_pass * P, at + j * P
    Z_AT, G_AT, I_AT = 3 * DNW, 4 * DNW, 4 * DNW + HGW
    dn = [tile_of("conv", j, C_DN, NC // 2, 0) for j in range(NC // 2)]
    zz = [tile_of("plain", j, C_Z, 2, Z_AT) for j in range(2)]
    SLOTS = [dn[0], zz[0], dn[1], tile_of("plain", 0, C_HI, 1, I_AT), dn[2], tile_of("chan", 0, C_HQ, 1, 0),
             dn[3], zz[1], dn[4], tile_of("plain", 0, C_HG, 1, G_AT), dn[5], tile_of("chan", 0, C_HF, 1, 2)]
    NS = len(SLOTS)
    NH = 2 * NS
    W_AB, W_P1, W_OUT = 6, 7, 7 + 2 * NS
    W_FF = W_OUT + KT
    SB_AT = 4 * DNW + 2 * HGW
    TM = SB_AT + SBW

    UNITS = []
    for hh in range(2):
        for g in range(2):
            blocks = list(range(4 * g + 3, -1, -1))
            for r, m in enumerate(blocks):
                UNITS.append((hh, g, m, max(m - 4 * g, 0) * P, r, len(blocks), m >= 4 * g))
    assert len(UNITS) == NH

    def before(items, k):
        return sum(1 for u in items[:k] if u)
    DIAG = [u[6] for u in UNITS]
    SUMS = [u[4] < u[5] - 1 for u in UNITS]
    STARTS = [u[6] and 0 < u[4] < u[5] - 1 for u in UNITS]
    ENDS = [u[4] == u[5] - 1 for u in UNITS]
    CONV = [SLOTS[k // 2][0] == "conv" for k in range(NH)]
    TOKM = [SLOTS[k // 2][0] != "chan" for k in range(NH)]
    nd, nsum, nstart, nend, nconv, ntok = (sum(v) for v in (DIAG, SUMS, STARTS, ENDS, CONV, TOKM))

    tm_dram = nc.dram_tensor("projected_tm", [T, TM], F32, kind="Internal").ap()
    cm_dram = nc.dram_tensor("projected_cm", [4, P, T], F32, kind="Internal").ap()

    w_in = a["w_in"][0].rearrange("(k p) n -> p k n", p=P)
    w_out = a["w_out"][0].rearrange("(k p) n -> p k n", p=P)
    w_gate = a["w_gate"][0].rearrange("(k p) n -> p k n", p=P)
    w_up = a["w_up"][0].rearrange("(k p) n -> p k n", p=P)
    w_down = a["w_down"][0].rearrange("(f p) n -> p f n", p=P)
    x_rows = a["x"][0].rearrange("(t p) d -> p t d", p=P)
    out_rows = out[0].rearrange("(t p) d -> p t d", p=P)

    with ExitStack() as ctx:
        sems = {}

        def sem(name):
            sems[name] = ctx.enter_context(nc.semaphore(name))

        def sb(name, shape, dt=F32):
            return ctx.enter_context(nc.sbuf_tensor(name, shape, dt))

        act_h = sb("act_h", [P, KT, T], F32R)
        act_l = sb("act_l", [P, KT, T], F32R)
        w_h = sb("w_h", [P, 2, KT, P], F32R)
        w_l = sb("w_l", [P, 2, KT, P], F32R)
        ff_h = sb("ff_h", [P, 2, T], F32R)
        ff_l = sb("ff_l", [P, 2, T], F32R)
        w_raw = sb("w_raw", [P, 2, KT, P])
        ident = sb("ident", [P, P])
        upto = sb("upto", [P, P])
        ones = sb("ones", [P, P])
        neg_after = sb("neg_after", [P, P])
        neg_ones = sb("neg_ones", [P, P])
        earlier = sb("earlier", [P, P])
        not_earlier = sb("not_earlier", [P, P])
        zeros = sb("zeros", [P, P])
        col_mask = sb("col_mask", [P, LEVELS, 64])
        pair_mask = sb("pair_mask", [P, LEVELS + 1, P])
        head_mask = sb("head_mask", [P, P])
        gain_row = sb("gain_row", [P, D])
        ssq = sb("ssq", [P, NT])
        lnv = sb("lnv", [P, NT])
        eps_col = sb("eps_col", [P, 1])
        rstd = sb("rstd", [P, NT])
        ab_tm = sb("ab_tm", [P, NT, 2 * DNH])
        small = {n: sb(n, [P, NT, DNH]) for n in ("g_all", "beta", "gc", "rest", "whole", "eg", "neg_be")}
        g_all, beta, gc, rest, whole, eg, neg_be = small.values()
        ab_s = sb("ab_s", [P, NT, 2 * DNH])
        dt_row, rate_log, rate = sb("dt_row", [P, DNH]), sb("rate_log", [P, DNH]), sb("rate", [P, DNH])
        r8, r16, r4 = sb("r8", [P, 2 * DNH]), sb("r16", [P, 16]), sb("r4", [P, DNH])
        AREA = 22096
        area = sb("area", [P, AREA])

        def carver():
            at = [0]

            def carve(*shape):
                n = 1
                for s in shape:
                    n *= s
                v = area[:, at[0]:at[0] + n]
                at[0] += n
                assert at[0] <= AREA, (at[0] / 256)
                if len(shape) == 2:
                    v = v.rearrange("p (a b) -> p a b", b=shape[1])
                if len(shape) == 3:
                    v = v.rearrange("p (a b c) -> p a b c", b=shape[1], c=shape[2])
                return v
            return carve

        carve = carver()
        x_sb = carve(NT, D)
        xn = carve(2, D)
        junk = carve(D)
        x_t = carve(2, T)
        gs = x_t[:, 0, :].rearrange("p (a b) -> p a b", a=2)
        ffv = x_t[:, 1, :].rearrange("p (a b) -> p a b", a=2)
        carve = carver()
        sb_t = carve(6, T)
        v_tm = carve(NT, SBW)
        k_one = carve(2, T)
        raw = carve(2, T + 3)
        az = carve(2, HALF)
        sp = carve(2, HALF)
        wt = carve(2, HALF)
        sp_sum = carve(HALF)
        cv = carve(2, HALF)
        cs = carve(2, HALF)
        cact = carve(2, HALF)
        tm_stage = carve(2, 4, P)
        ab_t = cv[:, :, :].rearrange("p a b -> p (a b)")
        cw_rows = carve(P)
        cw = carve(4, NC)
        o_stage = carve(2, 4, SBD)
        carve = carver()
        pin = carve(TM)
        qk = pin[:, 0:2 * DNW].rearrange("p (h c) -> p h c", c=P)
        qn, kn = qk[:, 0:DNH, :], qk[:, DNH:, :]
        vv = pin[:, 2 * DNW:3 * DNW].rearrange("p (h c) -> p h c", c=P)
        cin = carve(4, P)
        kb, kd, qd = (carve(DNH, P) for _ in range(3))
        kt, kbt, qt, qdt = (carve(DNH, P) for _ in range(4))
        span, dtr = carve(DNH, P), carve(DNH, P)
        mm_, at, rhs, vnew = (carve(DNH, P) for _ in range(4))
        tb = carve(2 * DNH, P).rearrange("p (z h) c -> p z h c", z=2)
        xy = carve(DNH, 64)
        hv = carve(HGW)
        state = carve(DNH, P)
        hls, hq, hk, hb = carve(4, P), carve(2, P), carve(2, P), carve(2, P)
        el = carve(8, P).rearrange("p (n g) c -> p n g c", g=2)
        qe = carve(8, P).rearrange("p (n g) c -> p n g c", g=2)
        ke = carve(8, P).rearrange("p (n g) c -> p n g c", g=2)
        sc = carve(4, P)
        qb, eb, kdc, kdt, hstate, htmp = (carve(2, P) for _ in range(6))
        gate, sq, mix = carve(D), carve(D), carve(D)
        banks = [ctx.enter_context(nc.psum_tensor(f"banks{i}", [P, 2, HALF], F32)) for i in range(4)]

        def bank(n):
            return banks[n // 2][:, n % 2, :]

        for name in ("consts", "gain_loaded", "small_loaded", "norm_ssq", "norm_ln", "norm_rstd", "norm_xn",
                     "norm_turned", "norm_h", "norm_l", "w_loaded0", "w_loaded1", "wh_ready", "wl_ready", "dense_done", "dense_evac",
                     "k_one_ready", "small_turned", "small_ready"):
            sem(name)
        for name in ("z_done", "z_abs", "z_exp", "z_ln", "sp_ready", "sp_masked", "sum_ready", "tri_done", "wt_ready",
                     "wt_masked", "av_done", "o_evac", "conv_step", "conv_done", "conv_abs", "conv_exp", "conv_ln", "conv_ls", "conv_sg",
                     "conv_act", "tm_turned", "tm_ready", "tm_stored0", "tm_stored1", "cm_stored", "sum_started", "k_zero"):
            sem(name)
        for n in range(NT // 2):
            sem(f"x_loaded{n}")

        def hold(e, n):
            e.tensor_copy(held[:, n:n + 1], eps_col[:, :])

        for name in """rows_loaded gains_loaded o_stored0 o_stored1 pin_loaded rest_loaded cin_loaded zeroed decay_dve decay_act
                decay_sums gup gr_done turned turned_copy m_turned t_turned t_copied hv_ready kk_done x_done xy d_done tt h_p ks_done kdt_done ho_done vn_done hs_done
                o_done su_done mt_done sq h_abs h_exp h_ln dn_ssq dn_ln dn_r zg_abs zg_exp zg_ln h_ls h_sg h_k0  a_cut 
                spans  h_b h_eb h_kd0 h_kd1 h_dl h_dabs h_el zg_ls zg_sg kdt mix_hg vn mix_dn mix_sb msq m_sums m_ln m_r
                act_high act_low t_init vb kd h_q h_qb h_kd at at0 h_ke gated hs_dec s_dec m_n fin dn_rq qkn scaled  a1 h_qe
                h_sc m ks r htmp hs_new s_new x_turned x1_ready gu_done ff_silu ff_mul ff_high ff_low down_done x_added
                out_ready out_stored""".split():
            sem(name)

        def absolute_value(e, dst, src):
            return e.tensor_scalar(dst.bitcast(I32), src.bitcast(I32), 0x7fffffff, None, ALU.bitwise_and)

        block = ctx.enter_context(nc.Block())

        def load_tile(e, w, b, src):
            e.wait_ge(sems["wl_ready"], BASE + w - 1)
            e.dma_start(w_raw[:, b], src).then_inc(sems[f"w_loaded{b}"], 16)

        def split_high(e, w, b, used=True):
            e.wait_ge(sems[f"w_loaded{b}"], BASE + 8 * (w - b) + 16)
            if used:
                e.wait_ge(sems["dense_done"], BASE + 2 * (w - 1))
            e.activation(w_h[:, b], w_raw[:, b], ACT.Copy).then_inc(sems["wh_ready"], 1)

        def split_low(e, w, b):
            e.wait_ge(sems["wh_ready"], BASE + w + 1)
            e.tensor_tensor(w_l[:, b], w_raw[:, b], w_h[:, b].bitcast(F32), ALU.subtract).then_inc(sems["wl_ready"], 1)

        def dense_half(e, w, b, th, dst):
            if th == 0:
                e.wait_ge(sems["wl_ready"], BASE + w + 1)
            e.wait_ge(sems["dense_evac"], BASE + 2 * w + th - 1)
            cols = slice(th * HALF, (th + 1) * HALF)
            for k in range(KT):
                e.matmul(dst, w_h[:, b, k], act_h[:, k, cols], start=(k == 0), stop=False)
                e.matmul(dst, w_h[:, b, k], act_l[:, k, cols], start=False, stop=False)
                mm = e.matmul(dst, w_l[:, b, k], act_h[:, k, cols], start=False, stop=(k == KT - 1))
            mm.then_inc(sems["dense_done"], 1)

        def norm_act(e, which):
            def high(n, b):
                e.wait_ge(sems["norm_turned"], BASE + which * NT + n + 1)
                e.activation(act_h[:, :, ds(n * P, P)], banks[b][:, :, :].rearrange("p a (k c) -> p (a k) c", c=P),
                             ACT.Copy).then_inc(sems["norm_h"], 1)

            for n in range(NT):
                if which == 0:
                    e.wait_ge(sems[f"x_loaded{n // 2}"], BASE + 16)
                else:
                    e.wait_ge(sems["x1_ready"], BASE + 2 * KT)
                e.activation(junk, x_sb[:, n, :], ACT.Square, accum_out=ssq[:, n:n + 1]).then_inc(sems["norm_ssq"], 1)
                if n >= 2:
                    high(n - 2, n % 2)
                if which == 0 and n == NT - 1:
                    split_high(e, 0, 0)
                e.wait_ge(sems["norm_ssq"], BASE + which * NT + n + 1)
                e.activation(lnv[:, n:n + 1], ssq[:, n:n + 1], ACT.Ln, scale=1.0 / D, bias=eps_col[:, 0:1]).then_inc(sems["norm_ln"], 1)
                e.wait_ge(sems["norm_ln"], BASE + which * NT + n + 1)
                e.activation(rstd[:, n:n + 1], lnv[:, ds(n, 1)], ACT.Exp, scale=-0.5).then_inc(sems["norm_rstd"], 1)
            for n in range(NT - 2, NT):
                high(n, n % 2)

        def norm_dve(e, which):
            e.wait_ge(sems["gain_loaded"], BASE + 16 * (which + 1))
            def scaled(n, b):
                e.wait_ge(sems["norm_rstd"], BASE + which * NT + n + 1)
                e.wait_ge(sems["norm_turned"], BASE + which * NT + n - 1)
                e.scalar_tensor_tensor(out=xn[:, b], in0=x_sb[:, n, :], scalar=rstd[:, ds(n, 1)], in1=gain_row[:, :],
                                            op0=ALU.mult, op1=ALU.mult).then_inc(sems["norm_xn"], 1)

            def low(n, b):
                e.wait_ge(sems["norm_h"], BASE + which * NT + n + 1)
                e.tensor_tensor(act_l[:, :, ds(n * P, P)], banks[b][:, :, :].rearrange("p a (k c) -> p (a k) c", c=P),
                                     act_h[:, :, ds(n * P, P)].bitcast(F32), ALU.subtract).then_inc(sems["norm_l"], 1)
            for b in range(2):
                scaled(b, b)
            with e.Fori(0, NT // 2 - 1) as i:
                for b in range(2):
                    low(2 * i + b, b)
                    scaled(2 * i + 2 + b, b)
            for b in range(2):
                low(NT - 2 + b, b)

        def norm_pe(e, which):
            with e.Fori(0, NT // 2) as i:
                for b in range(2):
                    n = 2 * i + b
                    e.wait_ge(sems["norm_xn"], BASE + which * NT + n + 1)
                    e.wait_ge(sems["norm_l"], BASE + which * NT + n - 1)
                    for k in range(KT):
                        mm = e.transpose(banks[b][:, k // 4, (k % 4) * P:(k % 4 + 1) * P], xn[:, b, k * P:(k + 1) * P], ident[:, :])
                    mm.then_inc(sems["norm_turned"], 1)

        held = sb("held", [P, 8])

        def masks(e):
            cleared = 0

            def select(v, op, base, pattern, cm, fill):
                nonlocal cleared
                cleared += 1
                e.wait_ge(sems["consts"], cleared)
                e.affine_select(out=v, in_=v, compare_op=op, fill=fill, base=base, pattern=pattern, channel_multiplier=cm).then_inc(sems["consts"], 1)

            for v, value in ((eps_col, EPS), (ident, 0.0)):
                cleared += 1
                e.memset(v[:], value).then_inc(sems["consts"], 1)
            cleared -= 1
            select(ident[:, :], ALU.not_equal, 0, [[1, P]], -1, 1.0)
            cleared += 1
            assert cleared == CONSTS_FIRST
            for name in sems:
                if name != "consts":
                    e.sem_inc(sems[name], BASE)
            for v, value in ((upto, 1.0), (neg_after, -1.0), (ones, 1.0), (earlier, 1.0), (not_earlier, 1.0), (zeros, 0.0), (neg_ones, -1.0),
                             (col_mask, 1.0), (pair_mask, 1.0), (head_mask, 1.0)):
                cleared += 1
                e.memset(v[:], value).then_inc(sems["consts"], 1)
            cleared -= 1
            select(upto[:, :], ALU.is_ge, 0, [[1, P]], -1, 0.0)
            select(earlier[:, :], ALU.is_gt, 0, [[1, P]], -1, 0.0)
            select(not_earlier[:, :], ALU.is_ge, 0, [[-1, P]], 1, 0.0)
            select(neg_after[:, :], ALU.is_ge, 0, [[-1, P]], 1, 0.0)
            for lv in range(LEVELS):
                s = 2 ** lv
                m = col_mask[:, lv, :].rearrange("p (b r) -> p b r", r=s)
                select(m, ALU.is_ge, 0, [[-2 * s, 64 // s], [0, s]], 1, 0.0)
                select(m, ALU.is_ge, s - 1, [[2 * s, 64 // s], [0, s]], -1, 0.0)
            for lv in range(LEVELS):
                h = P >> (lv + 1)
                m = pair_mask[:, lv, :].rearrange("p (b r) -> p b r", r=2 * h)
                nb = P // (2 * h)
                select(m, ALU.is_ge, -h, [[0, nb], [1, 2 * h]], 0, 0.0)
                select(m, ALU.is_ge, 0, [[-2 * h, nb], [0, 2 * h]], 1, 0.0)
                select(m, ALU.is_ge, h - 1, [[2 * h, nb], [0, 2 * h]], -1, 0.0)
            select(pair_mask[:, LEVELS, :], ALU.is_equal, 0, [[1, P]], -1, 0.0)
            m = head_mask[:, :].rearrange("p (b r) -> p b r", r=64)
            select(m, ALU.is_ge, 0, [[-64, 2], [0, 64]], 1, 0.0)
            select(m, ALU.is_ge, 63, [[64, 2], [0, 64]], -1, 0.0)
            return cleared + 1

        def in_tile(w):
            return w_in[:, :, ds(w * P, P)]

        def first_sync(e):
            with e.Fori(0, 3) as i:
                for b in range(2):
                    load_tile(e, 2 * i + b, b, in_tile(2 * i + b))
            load_tile(e, W_AB, 0, w_in[:, :, C_AB:C_AB + P])

        def first_pe(e):
            e.wait_ge(sems["small_loaded"], BASE + 16)
            e.transpose(bank(7)[:, 0:4 * NC], cw_rows[0:4 * NC, :], ident[0:4 * NC, 0:4 * NC]).then_inc(sems["small_turned"], 1)
            with e.Fori(0, 3) as i:
                for b in range(2):
                    for th in range(2):
                        dense_half(e, 2 * i + b, b, th, bank(th))
            for th in range(2):
                dense_half(e, W_AB, 0, th, bank(th))
            for v in range(2):
                for th in range(2):
                    n = 2 * v + th
                    e.wait_ge(sems["dense_evac"], BASE + 2 * (4 + v) + th + 1)
                    if n >= 2:
                        e.wait_ge(sems["small_ready"], BASE + n)
                    for j in range(4):
                        mm = e.transpose(bank(2 + n % 2)[:, j * P:(j + 1) * P],
                                         sb_t[:, 4 + v, (4 * th + j) * P:(4 * th + j + 1) * P], ident[:, :])
                    mm.then_inc(sems["small_turned"], 1)
            e.wait_ge(sems["dense_evac"], BASE + 2 * W_AB + 2)
            for t in range(NT):
                mm = e.transpose(bank(4)[:, 8 * t:8 * t + 8], ab_t[0:8, t * P:(t + 1) * P], ident[0:8, 0:8])
            mm.then_inc(sems["small_turned"], 1)

        def first_act(e):
            with e.Fori(0, 3) as i:
                for b in range(2):
                    w = 2 * i + b
                    split_high(e, w + 1, 1 - b)
                    for th in range(2):
                        e.wait_ge(sems["dense_done"], BASE + 2 * w + th + 1)
                        e.activation(sb_t[:, w, th * HALF:(th + 1) * HALF], bank(th), ACT.Copy).then_inc(sems["dense_evac"], 1)
            split_high(e, W_P1, 1)
            for th in range(2):
                e.wait_ge(sems["dense_done"], BASE + 2 * W_AB + th + 1)
                e.activation(ab_t[0:8, th * HALF:(th + 1) * HALF], bank(th)[0:8, :], ACT.Copy).then_inc(sems["dense_evac"], 1)

        def first_pool(e):
            split_low(e, 0, 0)
            e.wait_ge(sems["norm_l"], BASE + NT)
            e.memset(k_one[:, :, :], 0.0).then_inc(sems["k_zero"], 1)
            e.memset(raw[:, :, 0:3], 0.0).then_inc(sems["k_zero"], 1)
            with e.Fori(0, 3) as i:
                for b in range(2):
                    split_low(e, 2 * i + b + 1, 1 - b)
            split_low(e, W_P1, 1)

        def first_dve(e):
            e.wait_ge(sems["small_turned"], BASE + 1)
            e.tensor_copy(cw[:, :, :], bank(7)[:, 0:4 * NC].rearrange("p (k c) -> p k c", c=NC)).then_inc(sems["small_ready"], 1)
            for v in range(2):
                for th in range(2):
                    n = 2 * v + th
                    e.wait_ge(sems["small_turned"], BASE + n + 2)
                    e.tensor_copy(v_tm[:, 4 * th:4 * th + 4, v * P:(v + 1) * P],
                                       bank(2 + n % 2).rearrange("p (t c) -> p t c", c=P)).then_inc(sems["small_ready"], 1)
            e.wait_ge(sems["small_turned"], BASE + 6)
            e.tensor_copy(ab_tm[:, :, :], bank(4)[:, 0:8 * NT].rearrange("p (t c) -> p t c", c=8)).then_inc(sems["small_ready"], 1)

        Z = [bank(2), bank(3)]
        O, TURN = bank(4), [bank(5), bank(6)]
        Ov = O[:, 0:4 * SBD].rearrange("p (j d) -> p j d", d=SBD)

        def lead_sync(e):
            with e.Fori(0, 2) as i:
                for s, (kind, col, per, at) in enumerate(SLOTS):
                    w = W_P1 + NS * i + s
                    load_tile(e, w, (W_P1 + s) % 2, w_in[:, :, ds(per * i + col, P)])

        def mix_pe(e):
            e.wait_ge(sems["small_ready"], BASE + 6)
            with e.Fori(0, 2) as i:
                def scores(k):
                    hh, g, m, c0, r, R, diag = UNITS[k]
                    if r == 0 and g == 0:
                        e.wait_ge(sems["k_one_ready"], BASE + 2 * i + hh + 1)
                    e.wait_ge(sems["wt_ready"], BASE + NH * i + k - 1)
                    e.matmul(Z[k % 2][:, c0:], k_one[:, hh, m * P:(m + 1) * P],
                                  sb_t[:, i, g * HALF + c0:(g + 1) * HALF], start=True, stop=True).then_inc(sems["z_done"], 1)

                def suffix(k):
                    hh, g, m, c0, r, R, diag = UNITS[k]
                    if diag:
                        e.wait_ge(sems["sp_masked"], BASE + nd * i + before(DIAG, k) + 1)
                    else:
                        e.wait_ge(sems["sp_ready"], BASE + NH * i + k + 1)
                    if r > 0:
                        e.wait_ge(sems["sum_ready"], BASE + nsum * i + before(SUMS, k))
                        c = c0 + P if diag else c0
                        e.matmul(Z[k % 2][:, c:], neg_ones[:, :], sp_sum[:, c:], start=False, stop=True,
                                 skip_group_check=True)
                    e.matmul(Z[k % 2][:, c0:], neg_after[:, :], sp[:, k % 2, c0:], start=False, stop=True,
                                  skip_group_check=True).then_inc(sems["tri_done"], 1)

                def weigh(k):
                    hh, g, m, c0, r, R, diag = UNITS[k]
                    if diag:
                        e.wait_ge(sems["wt_masked"], BASE + nd * i + before(DIAG, k) + 1)
                    else:
                        e.wait_ge(sems["wt_ready"], BASE + NH * i + k + 1)
                    if r == 0:
                        e.wait_ge(sems["o_evac"], BASE + nend * i + before(ENDS, k))
                    for j in range(c0 // P, 4):
                        mm = e.matmul(Ov[:, j, :], wt[:, k % 2, j * P:(j + 1) * P], v_tm[:, m, ds(i * P + hh * SBD, SBD)],
                                      start=(r == 0), stop=(r == R - 1), skip_group_check=True)
                    mm.then_inc(sems["av_done"], 1)

                def turn(k):
                    n = ntok * i + before(TOKM, k)
                    e.wait_ge(sems["tm_ready"], BASE + n - 1)
                    if CONV[k]:
                        e.wait_ge(sems["conv_act"], BASE + nconv * i + before(CONV, k) + 1)
                        src = cact[:, k % 2, :]
                    else:
                        e.wait_ge(sems["dense_evac"], BASE + 2 * W_P1 + NH * i + k + 1)
                        src = raw[:, k // 2 % 2, 3 + (k % 2) * HALF:3 + (k % 2 + 1) * HALF]
                    for j in range(4):
                        mm = e.transpose(TURN[k % 2][:, j * P:(j + 1) * P], src[:, j * P:(j + 1) * P], ident[:, :])
                    mm.then_inc(sems["tm_turned"], 1)

                for k in range(NH + 2):
                    if k < NH:
                        scores(k)
                        dense_half(e, W_P1 + NS * i + k // 2, (W_P1 + k // 2) % 2, k % 2, bank(k % 2))
                        suffix(k)
                    if 1 <= k <= NH:
                        weigh(k - 1)
                    if k >= 2 and TOKM[k - 2]:
                        turn(k - 2)

        def mix_act(e):
            e.wait_ge(sems["k_zero"], BASE + 2)
            with e.Fori(0, 2) as i:
                for hh in range(2):
                    e.wait_ge(sems["z_done"], BASE + NH * i)
                    rows = slice(hh * SBD, (hh + 1) * SBD)
                    e.activation(k_one[rows, hh, :], sb_t[rows, 2 + i, :], ACT.Copy, scale=SBD ** -0.5).then_inc(sems["k_one_ready"], 1)

                def take(k):
                    w0 = 2 * W_P1 + NH * i + k
                    s = k // 2
                    e.wait_ge(sems["dense_done"], BASE + w0 + 1)
                    e.wait_ge(sems["cm_stored"], BASE + 16 * (2 * i + sum(u[0] == "chan" for u in SLOTS[:max(s - 1, 0)])))
                    e.wait_ge(sems["conv_done"], BASE + nconv * i + before(CONV, 2 * max(s - 1, 0)))
                    e.wait_ge(sems["tm_turned"], BASE + ntok * i + before(TOKM, 2 * max(s - 1, 0)))
                    e.activation(raw[:, s % 2, 3 + (k % 2) * HALF:3 + (k % 2 + 1) * HALF], bank(k % 2), ACT.Copy).then_inc(sems["dense_evac"], 1)

                def store_chan(k):
                    s = k // 2
                    e.wait_ge(sems["dense_evac"], BASE + 2 * W_P1 + NH * i + k + 1)
                    e.dma_start(cm_dram[ds(i + SLOTS[s][3], 1), :, :].rearrange("a p t -> p (a t)"),
                                     raw[:, s % 2, 3:3 + T]).then_inc(sems["cm_stored"], 16)

                def z_soft(k):
                    hh, g, m, c0, r, R, diag = UNITS[k]
                    n = NH * i + k
                    e.wait_ge(sems["z_abs"], BASE + n + 1)
                    e.activation(az[:, k % 2, c0:], az[:, k % 2, c0:], ACT.Exp, scale=-1.0).then_inc(sems["z_exp"], 1)
                    e.wait_ge(sems["z_exp"], BASE + n + 1)
                    e.activation(az[:, k % 2, c0:], az[:, k % 2, c0:], ACT.Ln, bias=1.0).then_inc(sems["z_ln"], 1)

                def weights(k):
                    c0 = UNITS[k][3]
                    n = NH * i + k
                    e.wait_ge(sems["tri_done"], BASE + n + 1)
                    e.wait_ge(sems["av_done"], BASE + n - 1)
                    e.activation(wt[:, k % 2, c0:], Z[k % 2][:, c0:], ACT.Exp).then_inc(sems["wt_ready"], 1)

                def store_tok(k):
                    n = ntok * i + before(TOKM, k)
                    kind, col, per, at = SLOTS[k // 2]
                    step = (NC // 2) * P if kind == "conv" else per
                    e.wait_ge(sems["tm_ready"], BASE + n + 1)
                    e.dma_start(tm_dram[(k % 2) * HALF:(k % 2 + 1) * HALF, ds(step * i + at, P)]
                                     .rearrange("(j p) c -> p j c", p=P), tm_stage[:, k % 2]).then_inc(sems[f"tm_stored{k % 2}"], 16)

                def store_out(k):
                    hh, g = UNITS[k][:2]
                    n = before(ENDS, k)
                    e.wait_ge(sems["o_evac"], BASE + nend * i + n + 1)
                    e.dma_start(tm_dram[g * HALF:(g + 1) * HALF, ds(i * P + SB_AT + hh * SBD, SBD)]
                                     .rearrange("(j p) c -> p j c", p=P), o_stage[:, n % 2]).then_inc(sems[f"o_stored{n % 2}"], 16)

                def silu(k):
                    n = nconv * i + before(CONV, k)
                    e.wait_ge(sems["conv_abs"], BASE + n + 1)
                    e.activation(cs[:, k % 2, :], cs[:, k % 2, :], ACT.Exp, scale=-1.0).then_inc(sems["conv_exp"], 1)
                    e.wait_ge(sems["conv_exp"], BASE + n + 1)
                    e.activation(cs[:, k % 2, :], cs[:, k % 2, :], ACT.Ln, bias=1.0).then_inc(sems["conv_ln"], 1)
                    e.wait_ge(sems["conv_ls"], BASE + n + 1)
                    e.activation(cs[:, k % 2, :], cs[:, k % 2, :], ACT.Exp).then_inc(sems["conv_sg"], 1)

                for k in range(NH + 5):
                    if 1 <= k <= NH:
                        take(k - 1)
                    if k < NH:
                        z_soft(k)
                        if k % 2 == 0:
                            split_high(e, W_P1 + NS * i + k // 2 + 1, (W_P1 + k // 2 + 1) % 2)
                    if 1 <= k <= NH:
                        weights(k - 1)
                        if not TOKM[k - 1] and k % 2 == 0:
                            store_chan(k - 1)
                    if 4 <= k < NH + 4 and TOKM[k - 4]:
                        store_tok(k - 4)
                    if 3 <= k < NH + 3 and ENDS[k - 3]:
                        store_out(k - 3)
                    if 1 <= k <= NH and CONV[k - 1]:
                        silu(k - 1)

        def mixed_to_dram(e):
            e.wait_ge(sems["cm_stored"], BASE + 16 * 4)
            for half in range(2):
                e.wait_ge(sems[f"tm_stored{half}"], BASE + 16 * ntok)
                e.wait_ge(sems[f"o_stored{half}"], BASE + 16 * nend)
            e.wait_ge(sems["av_done"], BASE + 2 * NH)

        def mix_pool(e):
            with e.Fori(0, 2) as i:
                def mask_sp(k):
                    hh, g, m, c0, r, R, diag = UNITS[k]
                    e.wait_ge(sems["sp_ready"], BASE + NH * i + k + 1)
                    e.tensor_tensor(sp[:, k % 2, c0:c0 + P], sp[:, k % 2, c0:c0 + P], earlier[:, :], ALU.mult).then_inc(sems["sp_masked"], 1)

                def add_sum(k):
                    hh, g, m, c0, r, R, diag = UNITS[k]
                    n = nsum * i + before(SUMS, k)
                    e.wait_ge(sems["tri_done"], BASE + NH * i + k + 1)
                    if diag:
                        e.wait_ge(sems["sp_masked"], BASE + nd * i + before(DIAG, k) + 1)
                        new = e.tensor_tensor(sp_sum[:, c0:c0 + P], sp[:, k % 2, c0:c0 + P], ones[:, :], ALU.mult)
                        if r == 0:
                            new.then_inc(sems["sum_ready"], 1)
                            return
                        new.then_inc(sems["sum_started"], 1)
                        c0 += P
                        e.wait_ge(sems["sum_started"], BASE + nstart * i + before(STARTS, k) + 1)
                    e.wait_ge(sems["sum_ready"], BASE + n)
                    e.tensor_tensor(sp_sum[:, c0:], sp_sum[:, c0:], sp[:, k % 2, c0:], ALU.add).then_inc(sems["sum_ready"], 1)

                for k in range(NH):
                    if k % 2 == 0:
                        split_low(e, W_P1 + NS * i + k // 2 + 1, (W_P1 + k // 2 + 1) % 2)
                    if DIAG[k]:
                        mask_sp(k)
                    if SUMS[k]:
                        add_sum(k)

        def mix_dve(e):
            with e.Fori(0, 2) as i:
                def absolute(k):
                    hh, g, m, c0, r, R, diag = UNITS[k]
                    e.wait_ge(sems["z_done"], BASE + NH * i + k + 1)
                    e.wait_ge(sems["sp_ready"], BASE + NH * i + k - 1)
                    absolute_value(e, az[:, k % 2, c0:], Z[k % 2][:, c0:]).then_inc(sems["z_abs"], 1)

                def softplus(k):
                    hh, g, m, c0, r, R, diag = UNITS[k]
                    n = NH * i + k
                    e.wait_ge(sems["z_ln"], BASE + n + 1)
                    e.wait_ge(sems["tri_done"], BASE + n - 1)
                    if k >= 2 and SUMS[k - 2]:
                        e.wait_ge(sems["sum_ready"], BASE + nsum * i + before(SUMS, k - 1))
                    e.scalar_tensor_tensor(out=sp[:, k % 2, c0:], in0=Z[k % 2][:, c0:], scalar=0.0, in1=az[:, k % 2, c0:],
                                                op0=ALU.max, op1=ALU.add).then_inc(sems["sp_ready"], 1)

                def convolve(k):
                    s = k // 2
                    n = nconv * i + before(CONV, k)
                    ch = (NC // 2) * i + (SLOTS[s][1] - C_DN) // P
                    at = (k % 2) * HALF
                    e.wait_ge(sems["dense_evac"], BASE + 2 * W_P1 + NH * i + k + 1)
                    e.wait_ge(sems["conv_act"], BASE + n - 1)
                    e.tensor_scalar(cv[:, k % 2], raw[:, s % 2, at + 3:at + 3 + HALF], cw[:, 3, ds(ch, 1)], None, ALU.mult).then_inc(sems["conv_step"], 1)
                    for tap in range(2, -1, -1):
                        e.wait_ge(sems["conv_step"], BASE + 3 * n + 3 - tap)
                        ins = e.scalar_tensor_tensor(out=cv[:, k % 2], in0=raw[:, s % 2, at + tap:at + tap + HALF],
                                                     scalar=cw[:, tap, ds(ch, 1)], in1=cv[:, k % 2], op0=ALU.mult, op1=ALU.add)
                        ins.then_inc(sems["conv_step" if tap else "conv_done"], 1)

                def conv_abs(k):
                    n = nconv * i + before(CONV, k)
                    e.wait_ge(sems["conv_done"], BASE + n + 1)
                    absolute_value(e, cs[:, k % 2, :], cv[:, k % 2, :]).then_inc(sems["conv_abs"], 1)

                def conv_gate(k):
                    n = nconv * i + before(CONV, k)
                    e.wait_ge(sems["conv_ln"], BASE + n + 1)
                    e.scalar_tensor_tensor(out=cs[:, k % 2], in0=cv[:, k % 2], scalar=0.0, in1=cs[:, k % 2],
                                                op0=ALU.min, op1=ALU.subtract).then_inc(sems["conv_ls"], 1)

                def conv_silu(k):
                    n = nconv * i + before(CONV, k)
                    e.wait_ge(sems["conv_sg"], BASE + n + 1)
                    e.wait_ge(sems["tm_turned"], BASE + ntok * i + before(TOKM, max(k - 1, 0)))
                    e.tensor_tensor(cact[:, k % 2], cv[:, k % 2], cs[:, k % 2], ALU.mult).then_inc(sems["conv_act"], 1)

                def stage_tok(k):
                    n = ntok * i + before(TOKM, k)
                    e.wait_ge(sems["tm_turned"], BASE + n + 1)
                    e.wait_ge(sems[f"tm_stored{k % 2}"], BASE + 16 * (ntok // 2 * i + before(TOKM, k) // 2))
                    e.tensor_copy(tm_stage[:, k % 2], TURN[k % 2].rearrange("p (j c) -> p j c", c=P)).then_inc(sems["tm_ready"], 1)

                def mask_wt(k):
                    hh, g, m, c0, r, R, diag = UNITS[k]
                    e.wait_ge(sems["wt_ready"], BASE + NH * i + k + 1)
                    hold(e, k % 2)
                    e.copy_predicated(wt[:, k % 2, c0:c0 + P], not_earlier[:, :].bitcast(I32), zeros[:, :]).then_inc(sems["wt_masked"], 1)

                def take_out(k):
                    hh, g, m, c0, r, R, diag = UNITS[k]
                    e.wait_ge(sems["av_done"], BASE + NH * i + k + 1)
                    n = before(ENDS, k)
                    e.wait_ge(sems[f"o_stored{n % 2}"], BASE + 16 * (nend // 2 * i + n // 2))
                    e.tensor_copy(o_stage[:, n % 2], Ov[:, :, :]).then_inc(sems["o_evac"], 1)

                for k in range(NH + 4):
                    if k < NH:
                        absolute(k)
                    if 1 <= k <= NH and DIAG[k - 1]:
                        mask_wt(k - 1)
                    if 1 <= k <= NH and CONV[k - 1]:
                        convolve(k - 1)
                        conv_abs(k - 1)
                    if k < NH:
                        softplus(k)
                    if 3 <= k < NH + 3 and TOKM[k - 3]:
                        stage_tok(k - 3)
                    if 1 <= k <= NH and CONV[k - 1]:
                        conv_gate(k - 1)
                    if 2 <= k <= NH + 1 and ENDS[k - 2]:
                        take_out(k - 2)
                    if 1 <= k <= NH and CONV[k - 1]:
                        conv_silu(k - 1)

        def decay_dve(e):
            e.wait_ge(sems["small_ready"], BASE + 6)
            e.wait_ge(sems["rows_loaded"], BASE + 32)
            e.tensor_tensor(ab_tm[:, :, 0:DNH], ab_tm[:, :, 0:DNH], dt_row[:, :].unsqueeze(1).to_broadcast([P, NT, DNH]),
                                 ALU.add).then_inc(sems["decay_dve"], 1)
            e.wait_ge(sems["decay_dve"], BASE + 1)
            absolute_value(e, ab_s[:, :, :], ab_tm[:, :, :]).then_inc(sems["decay_dve"], 1)
            e.wait_ge(sems["decay_act"], BASE + 3)
            e.scalar_tensor_tensor(out=g_all[:, :, :], in0=ab_tm[:, :, 0:DNH], scalar=0.0, in1=ab_s[:, :, 0:DNH],
                                        op0=ALU.max, op1=ALU.add).then_inc(sems["decay_dve"], 1)
            e.scalar_tensor_tensor(out=beta[:, :, :], in0=ab_tm[:, :, DNH:], scalar=0.0, in1=ab_s[:, :, DNH:],
                                        op0=ALU.min, op1=ALU.subtract).then_inc(sems["decay_dve"], 1)
            e.wait_ge(sems["decay_dve"], BASE + 3)
            e.scalar_tensor_tensor(out=g_all[:, :, :], in0=g_all[:, :, :], scalar=-1.0,
                                        in1=rate[:, :].unsqueeze(1).to_broadcast([P, NT, DNH]), op0=ALU.mult, op1=ALU.mult).then_inc(sems["decay_dve"], 1)
            e.wait_ge(sems["decay_sums"], BASE + 1)
            e.tensor_copy(gc[:, :, :], bank(0)[:, 0:NT * DNH].rearrange("p (t h) -> p t h", h=DNH)).then_inc(sems["decay_dve"], 1)
            e.tensor_copy(rest[:, :, :], bank(0)[:, NT * DNH:2 * NT * DNH].rearrange("p (t h) -> p t h", h=DNH)).then_inc(sems["decay_dve"], 1)
            e.wait_ge(sems["decay_act"], BASE + 5)
            e.wait_ge(sems["decay_dve"], BASE + 7)
            e.tensor_tensor(rest[:, :, :], rest[:, :, :], gc[:, :, :], ALU.subtract).then_inc(sems["decay_dve"], 1)
            e.wait_ge(sems["decay_act"], BASE + 6)
            e.scalar_tensor_tensor(out=neg_be[:, :, :], in0=beta[:, :, :], scalar=-1.0, in1=eg[:, :, :],
                                        op0=ALU.mult, op1=ALU.mult).then_inc(sems["decay_dve"], 1)

        def decay_act(e):
            e.wait_ge(sems["rows_loaded"], BASE + 32)
            e.activation(rate[:, :], rate_log[:, :], ACT.Exp).then_inc(sems["decay_act"], 1)
            e.wait_ge(sems["decay_dve"], BASE + 2)
            e.activation(ab_s[:, :, :], ab_s[:, :, :], ACT.Exp, scale=-1.0).then_inc(sems["decay_act"], 1)
            e.wait_ge(sems["decay_act"], BASE + 2)
            e.activation(ab_s[:, :, :], ab_s[:, :, :], ACT.Ln, bias=1.0).then_inc(sems["decay_act"], 1)
            e.wait_ge(sems["decay_dve"], BASE + 4)
            e.activation(beta[:, :, :], beta[:, :, :], ACT.Exp).then_inc(sems["decay_act"], 1)
            e.wait_ge(sems["decay_dve"], BASE + 7)
            e.activation(whole[:, :, :], rest[:, :, :], ACT.Exp).then_inc(sems["decay_act"], 1)
            e.activation(eg[:, :, :], gc[:, :, :], ACT.Exp).then_inc(sems["decay_act"], 1)
            e.wait_ge(sems["decay_dve"], BASE + 8)
            e.activation(rest[:, :, :], rest[:, :, :], ACT.Exp).then_inc(sems["decay_act"], 1)

        def decay_pe(e):
            e.wait_ge(sems["decay_dve"], BASE + 5)
            e.wait_ge(sems["dense_evac"], BASE + 2 * W_OUT)
            e.wait_ge(sems["tm_ready"], BASE + 2 * ntok)
            e.matmul(bank(0)[:, 0:NT * DNH], upto[:, :], g_all[:, :, :], start=True, stop=True)
            e.matmul(bank(0)[:, NT * DNH:2 * NT * DNH], ones[:, :], g_all[:, :, :], start=True, stop=True).then_inc(sems["decay_sums"], 1)

        def per_head(v, t, n=DNH, width=P):
            return v[:, t, :].unsqueeze(2).to_broadcast([P, n, width])

        def heads(v):
            return v.rearrange("p (h c) -> p h c", c=P)

        def right(v, s):
            return v.rearrange("p h (b z r) -> p (h b) z r", z=2, r=s)[:, :, 1, :]

        def blocks(v, s):
            return v.rearrange("p h (b r) -> p (h b) r", r=s)

        NX = LEVELS
        NU = LEVELS - 1

        def pipeline(e, head, body):
            head(0)
            with e.Fori(0, NT - 1) as t:
                body(t, True)
            body(NT - 1, False)

        def mixer_sync(e):
            def load_channels(u):
                e.dma_start(cin[:, :, :], cm_dram[:, :, ds(u * P, P)].rearrange("a p c -> p a c")).then_inc(sems["cin_loaded"], 16)

            def load_rows(u):
                e.dma_start(pin[:, 0:Z_AT], tm_dram[ds(u * P, P), 0:Z_AT]).then_inc(sems["pin_loaded"], 16)
                e.dma_start(pin[:, Z_AT:], tm_dram[ds(u * P, P), Z_AT:]).then_inc(sems["rest_loaded"], 16)

            load_channels(0)
            load_rows(0)
            with e.Fori(0, NT - 1) as t:
                e.wait_ge(sems["h_q"], BASE + t + 1)
                load_channels(t + 1)
                e.wait_ge(sems["zg_ls"], BASE + t + 1)
                e.wait_ge(sems["gated"], BASE + 2 * t + 1)
                load_rows(t + 1)

        def mixer_pe(e):
            def decays(u):
                e.wait_ge(sems["gup"], BASE + u + 1)
                e.matmul(bank(7), ones[:, :], span[:, :, :], start=True, stop=True).then_inc(sems["gr_done"], 1)

            def pack(t, lv):
                e.wait_ge(sems["tt"], BASE + NX * t + lv)
                e.wait_ge(sems["turned_copy"], BASE + 4 * t + 4)
                for h in range(DNH):
                    mm = e.matmul(bank(2)[:, h * P:(h + 1) * P], mm_[:, h, :], tb[:, 1, h, :], start=True, stop=True)
                mm.then_inc(sems["x_done"], 1)

            def turn(t, lv):
                if lv == 0:
                    e.wait_ge(sems["xy"], BASE + NX * t + 1)
                else:
                    e.wait_ge(sems["t_copied"], BASE + NU * t + lv)
                for h in range(DNH):
                    mm = e.transpose(bank(5)[:, h * P:(h + 1) * P], tb[:, 1, h, :], ident[:, :])
                mm.then_inc(sems["t_turned"], 1)

            def head(u):
                free = (("mix_hg", u), ("kdt", u), ("htmp", u), ("tt", NX * u))
                for n, (src, name, count) in enumerate(((kn, "qkn", u), (kb, "scaled", 2 * u), (qn, "qkn", u), (qd, "scaled", 2 * u + 1))):
                    e.wait_ge(sems[name], BASE + count + 1)
                    e.wait_ge(sems[free[n][0]], BASE + free[n][1])
                    for h in range(DNH):
                        mm = e.transpose(bank(n)[:, h * P:(h + 1) * P], src[:, h, :], ident[:, :])
                    mm.then_inc(sems["turned"], 1)
                e.wait_ge(sems["ks"], BASE + u)
                e.wait_ge(sems["turned_copy"], BASE + 4 * u + 2)
                for h in range(DNH):
                    mm = e.matmul(bank(4)[:, h * P:(h + 1) * P], kbt[:, h, :], kt[:, h, :], start=True, stop=True)
                mm.then_inc(sems["kk_done"], 1)
                e.wait_ge(sems["mix_dn"], BASE + u)
                e.wait_ge(sems["turned_copy"], BASE + 4 * u + 3)
                for h in range(DNH):
                    mm = e.matmul(bank(6)[:, h * P:(h + 1) * P], kt[:, h, :], qt[:, h, :], start=True, stop=True)
                mm.then_inc(sems["kk_done"], 1)

                e.wait_ge(sems["vn"], BASE + u)
                e.wait_ge(sems["m"], BASE + u + 1)
                for h in range(DNH):
                    mm = e.transpose(bank(5)[:, h * P:(h + 1) * P], mm_[:, h, :], ident[:, :])
                mm.then_inc(sems["m_turned"], 1)
                e.wait_ge(sems["s_new"], BASE + u)
                for h in range(DNH):
                    mm = e.matmul(bank(4)[:, h * P:(h + 1) * P], kt[:, h, :], state[:, h, :], start=True, stop=True)
                mm.then_inc(sems["ks_done"], 1)
                pack(u, 1); turn(u, 0)

            def body(t, more):
                def update(lv):
                    e.wait_ge(sems["xy"], BASE + NX * t + lv + 1)
                    e.wait_ge(sems["t_copied"], BASE + NU * t + lv)
                    for h in range(DNH):
                        mm = e.matmul(bank(3)[:, h * 64:(h + 1) * 64], tb[:, 0, h, :], xy[:, h, :], start=True, stop=True)
                    mm.then_inc(sems["d_done"], 1)

                def scores(lv):
                    e.wait_ge(sems["h_qe"], BASE + 2 * t + lv // 4 + 1)
                    e.wait_ge(sems["h_ke"], BASE + (2 * t + lv // 4 + 1))
                    if lv == 0:
                        e.wait_ge(sems["act_low"], BASE + 2 * t)
                    elif lv == 1:
                        e.wait_ge(sems["at0"], BASE + t + 1)
                    else:
                        e.wait_ge(sems["h_sc"], BASE + 8 * t + lv - 1)
                    for h in range(4):
                        rows = slice(h % 2 * 64, h % 2 * 64 + 64)
                        mm = e.matmul(banks[3 * (lv % 2)][:, h % 2, h // 2 * P:(h // 2 + 1) * P], ke[rows, lv % 4, h // 2, :],
                                      qe[rows, lv % 4, h // 2, :], start=True, stop=True)
                    mm.then_inc(sems["h_p"], 1)

                update(1); scores(0)
                pack(t, 2); turn(t, 1); scores(1); update(2); scores(2)
                pack(t, 3); turn(t, 2); scores(3); update(3)
                pack(t, 4); turn(t, 3); update(4); scores(4)
                pack(t, 5); turn(t, 4); scores(5); update(5); scores(6)
                pack(t, 6); turn(t, 5); scores(7); update(6)
                e.wait_ge(sems["h_sc"], BASE + 8 * t + 8)
                e.wait_ge(sems["h_kd"], BASE + t + 1)
                for g in range(2):
                    mm = e.transpose(bank(1)[:, g * P:(g + 1) * P], kdc[:, g, :], ident[:, :])
                mm.then_inc(sems["kdt_done"], 1)
                e.wait_ge(sems["h_qb"], BASE + t + 1)
                e.wait_ge(sems["hv_ready"], BASE + t + 1)
                e.wait_ge(sems["hs_new"], BASE + t)
                for g in range(2):
                    e.matmul(bank(0)[:, g * P:(g + 1) * P], qb[:, g, :], hstate[:, g, :], start=True, stop=True)
                    for hh in range(2):
                        h = 2 * g + hh
                        mm = e.matmul(bank(0)[:, h * 64:(h + 1) * 64], sc[:, 2 * hh + g, :], hv[:, h * 64:(h + 1) * 64],
                                      start=False, stop=True, skip_group_check=True)
                mm.then_inc(sems["ho_done"], 1)
                e.wait_ge(sems["r"], BASE + t + 1)
                e.wait_ge(sems["tt"], BASE + NX * t + NX)
                e.wait_ge(sems["t_copied"], BASE + NU * t + NU)
                for h in range(DNH):
                    mm = e.matmul(bank(5)[:, h * P:(h + 1) * P], tb[:, 1, h, :], rhs[:, h, :], start=True, stop=True)
                mm.then_inc(sems["vn_done"], 1)
                e.wait_ge(sems["kdt"], BASE + t + 1)
                e.wait_ge(sems["xy"], BASE + NX * t + NX)
                for g in range(2):
                    mm = e.matmul(bank(2)[:, g * P:(g + 1) * P], kdt[:, g, :], hv[:, g * P:(g + 1) * P], start=True, stop=True)
                mm.then_inc(sems["hs_done"], 1)
                if more:
                    decays(t + 1)
                e.wait_ge(sems["vn"], BASE + t + 1)
                e.wait_ge(sems["at"], BASE + t + 1)
                for h in range(DNH):
                    e.matmul(bank(6)[:, h * P:(h + 1) * P], qdt[:, h, :], state[:, h, :], start=True, stop=False)
                    mm = e.matmul(bank(6)[:, h * P:(h + 1) * P], at[:, h, :], vnew[:, h, :], start=False, stop=True)
                mm.then_inc(sems["o_done"], 1)
                e.wait_ge(sems["kd"], BASE + t + 1)
                if more:
                    e.wait_ge(sems["a1"], BASE + t + 2)
                for h in range(DNH):
                    mm = e.matmul(bank(7)[:, h * P:(h + 1) * P], kd[:, h, :], vnew[:, h, :], start=True, stop=True)
                mm.then_inc(sems["su_done"], 1)
                if more:
                    head(t + 1)
                    e.wait_ge(sems["turned_copy"], BASE + 4 * t + 6)
                else:
                    e.wait_ge(sems["act_low"], BASE + NT)
                    e.wait_ge(sems["ks"], BASE + t + 1)
                    dense_half(e, W_OUT, W_OUT % 2, 0, bank(4))
                    e.wait_ge(sems["mix_hg"], BASE + t + 1)
                    e.wait_ge(sems["kdt"], BASE + t + 1)
                e.wait_ge(sems["m_n"], BASE + t + 1)
                for n in range(2):
                    for k in range(4):
                        c = (4 * n + k) * P
                        mm = e.transpose(bank(n)[:, k * P:(k + 1) * P], mix[:, c:c + P], ident[:, :])
                    mm.then_inc(sems["mt_done"], 1)

            decays(0)
            pipeline(e, head, body)

        def mixer_act(e):
            def act(dst, src, func, name, **kw):
                e.activation(dst, src, func, **kw).then_inc(sems[name], 1)

            def squares(u, first):
                e.wait_ge(sems["pin_loaded"], BASE + 16 * u + 16)
                if not first:
                    e.wait_ge(sems["m_sums"], BASE + 3 * u - 5)
                act(sq[:, :], pin[:, 0:2 * DNW], ACT.Square, "sq")

            def softplus(u):
                e.wait_ge(sems["h_abs"], BASE + u + 1)
                act(hls[:, :, :], hls[:, :, :], ACT.Exp, "h_exp", scale=-1.0)
                e.wait_ge(sems["h_exp"], BASE + u + 1)
                act(hls[:, :, :], hls[:, :, :], ACT.Ln, "h_ln", bias=1.0)

            def lengths(u):
                e.wait_ge(sems["dn_ssq"], BASE + u + 1)
                act(r8[:, :], r8[:, :], ACT.Ln, "dn_ln", bias=eps_col[:, 0:1])
                e.wait_ge(sems["dn_ln"], BASE + u + 1)
                act(r8[:, :], r8[:, :], ACT.Exp, "dn_r", scale=-0.5)

            def sigmoids(u):
                e.wait_ge(sems["h_ls"], BASE + u + 1)
                e.wait_ge(sems["h_qe"], BASE + 2 * u)
                e.wait_ge(sems["h_qb"], BASE + u)
                e.wait_ge(sems["h_ke"], BASE + 2 * u)
                e.wait_ge(sems["h_kd"], BASE + u)
                act(hq[:, :, :], hls[:, 0:2, :], ACT.Exp, "h_sg")
                e.wait_ge(sems["h_k0"], BASE + u + 1)
                act(hk[:, :, :], hk[:, :, :], ACT.Exp, "h_sg")

            def turned_out(u, n):
                e.wait_ge(sems["turned"], BASE + 4 * u + n + 1)
                if n == 0:
                    e.wait_ge(sems["ks_done"], BASE + u)
                if n == 3:
                    e.wait_ge(sems["o_done"], BASE + u)
                act((kt, kbt, qt, qdt)[n][:, :, :], heads(bank(n)), ACT.Copy, "turned_copy")

            def spans(u):
                e.wait_ge(sems["a_cut"], BASE + 2 * u + 1)
                act(dtr[:, :, :], dtr[:, :, :], ACT.Exp, "spans")
                e.wait_ge(sems["a_cut"], BASE + 2 * u + 2)
                act(span[:, :, :], span[:, :, :], ACT.Exp, "spans", scale=-1.0)

            def head(u):
                squares(u, True)
                softplus(u)
                lengths(u)
                sigmoids(u)
                spans(u)
                for n in range(4):
                    turned_out(u, n)
                decays(u, 0)
                inverse(u, 0)

            def decays(t, q):
                e.wait_ge(sems["h_dabs"], BASE + 2 * t + q + 1)
                act(el[:, :, :, :], el[:, :, :, :], ACT.Exp, "h_el", scale=-1.0)

            def inverse(t, lv):
                e.wait_ge(sems["t_turned"], BASE + NU * t + lv + 1)
                act(tb[:, 0, :, :], heads(bank(5)), ACT.Copy, "t_copied")

            def body(t, more):
                e.wait_ge(sems["hs_dec"], BASE + t)
                act(eb[:, :, :], hb[:, :, :], ACT.Exp, "h_eb")
                e.wait_ge(sems["zg_abs"], BASE + t + 1)
                act(gate[:, SBW:], gate[:, SBW:], ACT.Exp, "zg_exp", scale=-1.0)
                inverse(t, 1)
                e.wait_ge(sems["zg_exp"], BASE + t + 1)
                act(gate[:, SBW:], gate[:, SBW:], ACT.Ln, "zg_ln", bias=1.0)
                e.wait_ge(sems["h_kd0"], BASE + t + 1)
                act(kdc[:, :, :], kdc[:, :, :], ACT.Exp, "h_kd1")
                inverse(t, 2)
                e.wait_ge(sems["zg_ls"], BASE + t + 1)
                act(gate[:, SBW:], gate[:, SBW:], ACT.Exp, "zg_sg")
                decays(t, 1)
                inverse(t, 3)
                if more:
                    squares(t + 1, False)
                inverse(t, 4)
                if more:
                    softplus(t + 1)
                inverse(t, 5)
                if more:
                    lengths(t + 1)
                    sigmoids(t + 1)
                e.wait_ge(sems["kdt_done"], BASE + t + 1)
                act(kdt[:, :, :], bank(1)[:, 0:2 * P].rearrange("p (g c) -> p g c", c=P), ACT.Copy, "kdt")
                e.wait_ge(sems["ho_done"], BASE + t + 1)
                e.wait_ge(sems["mt_done"], BASE + 2 * t)
                act(mix[:, SBW + DNW:], bank(0)[:, 0:HGW], ACT.Copy, "mix_hg")
                e.wait_ge(sems["vn_done"], BASE + t + 1)
                act(vnew[:, :, :], heads(bank(5)), ACT.Copy, "vn")
                if more:
                    spans(t + 1)
                e.wait_ge(sems["o_done"], BASE + t + 1)
                act(mix[:, SBW:SBW + DNW], bank(6), ACT.Copy, "mix_dn")
                if more:
                    turned_out(t + 1, 0)
                    turned_out(t + 1, 1)
                    e.wait_ge(sems["dn_ssq"], BASE + t + 2)
                e.wait_ge(sems["mix_dn"], BASE + t + 1)
                e.wait_ge(sems["mix_sb"], BASE + t + 1)
                act(sq[:, :], mix[:, :], ACT.Square, "msq")
                if more:
                    turned_out(t + 1, 2)
                    turned_out(t + 1, 3)
                e.wait_ge(sems["m_sums"], BASE + 3 * t + 3)
                act(r16[:, :], r16[:, :], ACT.Ln, "m_ln", scale=1.0 / 64, bias=eps_col[:, 0:1])
                e.wait_ge(sems["m_ln"], BASE + t + 1)
                act(r16[:, :], r16[:, :], ACT.Exp, "m_r", scale=-0.5)
                if more:
                    decays(t + 1, 0)
                    inverse(t + 1, 0)
                for n in range(2):
                    e.wait_ge(sems["mt_done"], BASE + 2 * t + n + 1)
                    act(act_h[:, 4 * n:4 * n + 4, ds(t * P, P)], heads(bank(n)), ACT.Copy, "act_high")
            pipeline(e, head, body)

        def mixer_pool(e):
            mixed_to_dram(e)
            for v in (sc[:, :, :], state[:, :, :], hstate[:, :, :]):
                e.memset(v, 0.0).then_inc(sems["zeroed"], 1)
            e.wait_ge(sems["gains_loaded"], BASE + 16 * (SBH + DNH + 4))
            e.tensor_copy(gate[:, 0:SBW], gain_row[:, 0:SBW]).then_inc(sems["zeroed"], 1)
            e.wait_ge(sems["decay_act"], BASE + 7)
            e.wait_ge(sems["decay_dve"], BASE + 9)

            def mul(dst, x, y, name):
                e.tensor_tensor(dst, x, y, ALU.mult).then_inc(sems[name], 1)

            def sums(u):
                e.wait_ge(sems["m"], BASE + u)
                mul(span[:, :, :], upto[:, :].unsqueeze(1).to_broadcast([P, DNH, P]), per_head(g_all, u), "gup")

            def unit(u):
                e.wait_ge(sems["vn_done"], BASE + u)
                mul(tb[:, 1, :, :], ident[:, :].unsqueeze(1).to_broadcast([P, DNH, P]),
                    ones[:, :].unsqueeze(1).to_broadcast([P, DNH, P]), "t_init")

            def head(u):
                sums(u)
                unit(u)

            def body(t, more):
                def keys(q):
                    e.wait_ge(sems["h_el"], BASE + 2 * t + q + 1)
                    e.wait_ge(sems["h_sg"], BASE + 2 * t + 2)
                    e.wait_ge(sems["h_p"], BASE + 8 * t + 4 * q)
                    mul(ke[:, :, :, :], el[:, :, :, :], hk[:, :, :].unsqueeze(1).to_broadcast([P, 4, 2, P]), "h_ke")

                keys(0)
                e.wait_ge(sems["pin_loaded"], BASE + 16 * t + 16)
                mul(rhs[:, :, :], vv, per_head(beta, t), "vb")
                e.wait_ge(sems["at0"], BASE + t + 1)
                mul(at[:, :, :], at[:, :, :], upto[:, :].unsqueeze(1).to_broadcast([P, DNH, P]), "at")
                e.wait_ge(sems["qkn"], BASE + t + 1)
                e.wait_ge(sems["su_done"], BASE + t)
                mul(kd[:, :, :], kn, per_head(rest, t), "kd")
                e.wait_ge(sems["hs_done"], BASE + t)
                e.wait_ge(sems["rest_loaded"], BASE + 16 * t + 16)
                mul(hv[:, :].rearrange("p (h c) -> p h c", c=P), pin[:, I_AT:I_AT + HGW].rearrange("p (h c) -> p h c", c=P),
                    ones[:, :].unsqueeze(1).to_broadcast([P, HGW // P, P]), "hv_ready")
                e.wait_ge(sems["mt_done"], BASE + 2 * t)
                mul(mix[:, 0:SBW].rearrange("p (h c) -> p h c", c=P), pin[:, SB_AT:].rearrange("p (h c) -> p h c", c=P),
                    ones[:, :].unsqueeze(1).to_broadcast([P, SBW // P, P]), "mix_sb")
                e.wait_ge(sems["zg_sg"], BASE + t + 1)
                mul(gate[:, SBW:SBW + DNW], gate[:, SBW:SBW + DNW], pin[:, Z_AT:Z_AT + DNW], "gated")
                keys(1)
                e.wait_ge(sems["h_kd1"], BASE + t + 1)
                mul(kdc[:, :, :], kdc[:, :, :], hk[:, :, :], "h_kd")
                e.wait_ge(sems["h_q"], BASE + t + 1)
                e.wait_ge(sems["h_eb"], BASE + t + 1)
                e.wait_ge(sems["ho_done"], BASE + t)
                mul(qb[:, :, :], hq[:, :, :], eb[:, :, :], "h_qb")
                if more:
                    sums(t + 1)
                e.wait_ge(sems["gated"], BASE + 2 * t + 1)
                mul(gate[:, SBW:], gate[:, SBW:], gain_row[:, SBW:], "gated")
                e.wait_ge(sems["ho_done"], BASE + t + 1)
                mul(hstate[:, :, :], hstate[:, :, :], eb[:, :, P - 1:P].to_broadcast([P, 2, P]), "hs_dec")
                if more:
                    unit(t + 1)
                e.wait_ge(sems["o_done"], BASE + t + 1)
                mul(state[:, :, :], state[:, :, :], per_head(whole, t), "s_dec")
                e.wait_ge(sems["msq"], BASE + t + 1)
                e.wait_ge(sems["gated"], BASE + 2 * t + 2)
                mul(mix[:, :], mix[:, :], gate[:, :], "fin")
            pipeline(e, head, body)

        def mixer_dve(e):
            def tt(dst, x, y, op, name):
                e.tensor_tensor(dst, x, y, op).then_inc(sems[name], 1)

            def ts(dst, x, v, op, name):
                e.tensor_scalar(dst, x, v, None, op).then_inc(sems[name], 1)

            def lengths(u):
                e.wait_ge(sems["cin_loaded"], BASE + 16 * u + 16)
                absolute_value(e, hls[:, :, :], cin[:, :, :]).then_inc(sems["h_abs"], 1)
                e.wait_ge(sems["sq"], BASE + u + 1)
                e.reduce_sum(r8[:, :], sq[:, :].rearrange("p (h c) -> p h c", c=P), AX.X).then_inc(sems["dn_ssq"], 1)

            def log_sigmoids(u):
                e.wait_ge(sems["h_ln"], BASE + u + 1)
                e.scalar_tensor_tensor(out=hls[:, :, :], in0=cin[:, :, :], scalar=0.0, in1=hls[:, :, :],
                                       op0=ALU.min, op1=ALU.subtract).then_inc(sems["h_ls"], 1)
                e.wait_ge(sems["h_ls"], BASE + u + 1)
                e.wait_ge(sems["h_ke"], BASE + 2 * u)
                e.wait_ge(sems["h_kd"], BASE + u)
                tt(hk[:, :, :], hls[:, 2:4, :], cin[:, 2:4, :], ALU.subtract, "h_k0")

            def unit_length(u):
                e.wait_ge(sems["dn_r"], BASE + u + 1)
                ts(r8[:, 0:DNH], r8[:, 0:DNH], float(P) ** -0.5, ALU.mult, "dn_rq")
                e.wait_ge(sems["dn_rq"], BASE + u + 1)
                tt(qk, qk, r8[:, :].unsqueeze(2).to_broadcast([P, 2 * DNH, P]), ALU.mult, "qkn")

            def scaled(u):
                e.wait_ge(sems["qkn"], BASE + u + 1)
                e.wait_ge(sems["r"], BASE + u)
                tt(kb[:, :, :], kn, per_head(beta, u), ALU.mult, "scaled")
                tt(qd[:, :, :], qn, per_head(eg, u), ALU.mult, "scaled")

            def running(u):
                e.wait_ge(sems["h_sg"], BASE + 2 * u + 1)
                tt(hq[:, :, :], hq[:, :, :], cin[:, 0:2, :], ALU.mult, "h_q")
                e.wait_ge(sems["h_eb"], BASE + u)
                for g in range(2):
                    e.tensor_tensor_scan(hb[:, g, :], ones[:, :], hls[:, 2 + g, :], 0.0, ALU.mult, ALU.add).then_inc(sems["h_b"], 1)

            def spans(u):
                e.wait_ge(sems["gr_done"], BASE + u + 1)
                tt(span[:, :, :], heads(bank(7)), per_head(gc, u), ALU.subtract, "a1")
                e.wait_ge(sems["a1"], BASE + u + 1)
                ts(dtr[:, :, :], span[:, :, :], 0.0, ALU.min, "a_cut")
                ts(span[:, :, :], span[:, :, :], 0.0, ALU.max, "a_cut")

            def spread(t, q):
                e.wait_ge(sems["h_ke"], BASE + 2 * t + q)
                e.wait_ge(sems["h_qe"], BASE + 2 * t + q)
                e.wait_ge(sems["h_b"], BASE + 2 * t + 2)
                for n in range(4):
                    lv = 4 * q + n
                    if lv == LEVELS:
                        tt(el[:, n, :, :], hb[:, :, :], hb[:, :, :], ALU.subtract, "h_dl")
                        continue
                    h = P >> (lv + 1)
                    v = hb[:, :, :].rearrange("p g (b r) -> p (g b) r", r=2 * h)
                    tt(el[:, n, :, :].rearrange("p g (b r) -> p (g b) r", r=2 * h), v,
                       v[:, :, h - 1:h].to_broadcast([P, P // h, 2 * h]), ALU.subtract, "h_dl")

            def positive(t, q):
                e.wait_ge(sems["h_dl"], BASE + 8 * t + 4 * q + 4)
                absolute_value(e, el[:, :, :, :], el[:, :, :, :]).then_inc(sems["h_dabs"], 1)

            def with_decay(u):
                e.wait_ge(sems["kk_done"], BASE + 2 * u + 1)
                e.wait_ge(sems["spans"], BASE + 2 * u + 2)
                tt(mm_[:, :, :], heads(bank(4)), span[:, :, :], ALU.mult, "m")

            def causal(u):
                e.wait_ge(sems["kk_done"], BASE + 2 * u + 2)
                e.wait_ge(sems["spans"], BASE + 2 * u + 1)
                tt(at[:, :, :], heads(bank(6)), dtr[:, :, :], ALU.mult, "at0")

            def queries(t, q):
                e.wait_ge(sems["h_el"], BASE + 2 * t + q + 1)
                e.wait_ge(sems["h_p"], BASE + 8 * t + 4 * q)
                e.wait_ge(sems["h_q"], BASE + t + 1)
                tt(qe[:, :, :, :], el[:, :, :, :], hq[:, :, :].unsqueeze(1).to_broadcast([P, 4, 2, P]), ALU.mult, "h_qe")

            def pack(t, lv):
                s = 2 ** lv
                mask = blocks(col_mask[:, lv:lv + 1, :], s).unsqueeze(1).to_broadcast([P, DNH, 64 // s, s])
                if lv == 0:
                    e.wait_ge(sems["m_turned"], BASE + t + 1)
                    e.wait_ge(sems["d_done"], BASE + NU * t)
                    src = bank(5)
                else:
                    e.wait_ge(sems["x_done"], BASE + NU * t + lv)
                    src = bank(2)
                tt(xy[:, :, :].rearrange("p h (b r) -> p h b r", r=s),
                   src.rearrange("p (h b z r) -> p h b z r", b=64 // s, z=2, r=s)[:, :, :, 1, :], mask, ALU.mult, "xy")

            def update(t, lv):
                s = 2 ** lv
                if lv == 0:
                    e.wait_ge(sems["xy"], BASE + NX * t + 1)
                    e.wait_ge(sems["t_init"], BASE + t + 1)
                    new = xy[:, :, :]
                else:
                    e.wait_ge(sems["d_done"], BASE + NU * t + lv)
                    new = bank(3)[:, 0:DNH * 64].rearrange("p (h c) -> p h c", c=64)
                dst = right(tb[:, 1, :, :], s)
                tt(dst, dst, blocks(new, s), ALU.subtract, "tt")

            def head(u):
                lengths(u)
                log_sigmoids(u)
                unit_length(u)
                scaled(u)
                spans(u)
                running(u)
                spread(u, 0)
                positive(u, 0)
                with_decay(u)
                pack(u, 0); update(u, 0)
                pack(u, 1)
                causal(u)
                queries(u, 0)

            def body(t, more):
                def take(lv):
                    e.wait_ge(sems["h_p"], BASE + 8 * t + lv + 1)
                    e.wait_ge(sems["h_sc"], BASE + 8 * t + lv)
                    if lv == 0:
                        e.wait_ge(sems["ho_done"], BASE + t)
                    hold(e, lv)
                    e.copy_predicated(sc[:, :, :].rearrange("p (z g) c -> p z g c", g=2),
                                      pair_mask[:, lv, :].bitcast(I32).unsqueeze(1).unsqueeze(1).to_broadcast([P, 2, 2, P]),
                                      banks[3 * (lv % 2)][:, :, 0:2 * P].rearrange("p z (g c) -> p z g c", c=P)).then_inc(sems["h_sc"], 1)

                update(t, 1)
                e.wait_ge(sems["fin"], BASE + t)
                e.wait_ge(sems["rest_loaded"], BASE + 16 * t + 16)
                absolute_value(e, gate[:, SBW:], pin[:, Z_AT:Z_AT + DNW + HGW]).then_inc(sems["zg_abs"], 1)
                pack(t, 2); take(0)
                e.wait_ge(sems["ks_done"], BASE + t + 1)
                e.wait_ge(sems["turned"], BASE + 4 * t + 2)
                tt(kb[:, :, :], heads(bank(4)), per_head(neg_be, t), ALU.mult, "ks")
                e.wait_ge(sems["kdt_done"], BASE + t)
                tt(kdc[:, :, :], hb[:, :, P - 1:P].to_broadcast([P, 2, P]), hb[:, :, :], ALU.subtract, "h_kd0")
                update(t, 2)
                e.wait_ge(sems["zg_ln"], BASE + t + 1)
                e.scalar_tensor_tensor(out=gate[:, SBW:], in0=pin[:, Z_AT:Z_AT + DNW + HGW], scalar=0.0, in1=gate[:, SBW:],
                                       op0=ALU.min, op1=ALU.subtract).then_inc(sems["zg_ls"], 1)
                pack(t, 3); take(1)
                spread(t, 1)
                update(t, 3)
                positive(t, 1)
                pack(t, 4); take(2)
                queries(t, 1)
                update(t, 4); take(3)
                pack(t, 5); take(4)
                if more:
                    lengths(t + 1)
                update(t, 5); take(5)
                pack(t, 6); take(6)
                e.wait_ge(sems["ks"], BASE + t + 1)
                e.wait_ge(sems["vb"], BASE + t + 1)
                tt(rhs[:, :, :], kb[:, :, :], rhs[:, :, :], ALU.add, "r")
                if more:
                    log_sigmoids(t + 1)
                update(t, 6); take(7)
                if more:
                    unit_length(t + 1)
                    scaled(t + 1)
                    running(t + 1)
                e.wait_ge(sems["hs_done"], BASE + t + 1)
                tt(htmp[:, :, :], bank(2)[:, 0:2 * P].rearrange("p (g c) -> p g c", c=P),
                   head_mask[:, :].unsqueeze(1).to_broadcast([P, 2, P]), ALU.mult, "htmp")
                if more:
                    spans(t + 1)
                e.wait_ge(sems["htmp"], BASE + t + 1)
                e.wait_ge(sems["hs_dec"], BASE + t + 1)
                tt(hstate[:, :, :], hstate[:, :, :], htmp[:, :, :], ALU.add, "hs_new")
                e.wait_ge(sems["su_done"], BASE + t + 1)
                e.wait_ge(sems["s_dec"], BASE + t + 1)
                tt(state[:, :, :], state[:, :, :], heads(bank(7)), ALU.add, "s_new")
                if more:
                    spread(t + 1, 0)
                    positive(t + 1, 0)
                    with_decay(t + 1)
                e.wait_ge(sems["msq"], BASE + t + 1)
                e.reduce_sum(r16[:, :], sq[:, :].rearrange("p (h c) -> p h c", c=64), AX.X).then_inc(sems["m_sums"], 1)
                e.wait_ge(sems["m_sums"], BASE + 3 * t + 1)
                pairs = r16[:, 4:4 + 2 * DNH].rearrange("p (h z) -> p h z", z=2)
                e.reduce_sum(r4[:, :], pairs, AX.X).then_inc(sems["m_sums"], 1)
                e.wait_ge(sems["m_sums"], BASE + 3 * t + 2)
                ts(pairs, r4[:, :].unsqueeze(2).to_broadcast([P, DNH, 2]), 0.5, ALU.mult, "m_sums")
                if more:
                    pack(t + 1, 0); update(t + 1, 0)
                e.wait_ge(sems["m_r"], BASE + t + 1)
                e.wait_ge(sems["fin"], BASE + t + 1)
                tt(mix[:, :].rearrange("p (h c) -> p h c", c=64), mix[:, :].rearrange("p (h c) -> p h c", c=64),
                   r16[:, :].unsqueeze(2).to_broadcast([P, 16, 64]), ALU.mult, "m_n")
                if more:
                    pack(t + 1, 1)
                    causal(t + 1)
                    queries(t + 1, 0)
                for n in range(2):
                    e.wait_ge(sems["act_high"], BASE + 2 * t + n + 1)
                    tt(act_l[:, 4 * n:4 * n + 4, ds(t * P, P)], heads(bank(n)),
                       act_h[:, 4 * n:4 * n + 4, ds(t * P, P)].bitcast(F32), ALU.subtract, "act_low")

            e.wait_ge(sems["zeroed"], BASE + 4)
            pipeline(e, head, body)

        def out_sync(e):
            with e.Fori(1, KT // 2) as i:
                for b in range(2):
                    w = W_OUT + 2 * i + b
                    load_tile(e, w, (W_OUT + b) % 2, w_out[:, :, ds((2 * i + b) * P, P)])

        def out_pe(e):
            e.wait_ge(sems["act_low"], BASE + 2 * NT)
            def tile(n, b, first):
                for th in range(first, 2):
                    dense_half(e, W_OUT + n, (W_OUT + b) % 2, th, bank(4 + th))
                for th in range(2):
                    e.wait_ge(sems["dense_evac"], BASE + 2 * (W_OUT + n) + th + 1)
                    e.wait_ge(sems["x1_ready"], BASE + 2 * n + th - 1)
                    for j in range(4):
                        c = th * HALF + j * P
                        mm = e.transpose(bank(2 + th)[:, j * P:(j + 1) * P], x_t[:, b, c:c + P], ident[:, :])
                    mm.then_inc(sems["x_turned"], 1)

            tile(0, 0, 1)
            tile(1, 1, 0)
            with e.Fori(1, KT // 2) as i:
                for b in range(2):
                    tile(2 * i + b, b, 0)

        def out_act(e):
            e.wait_ge(sems["act_low"], BASE + 2 * NT)
            with e.Fori(0, KT // 2) as i:
                for b in range(2):
                    w = W_OUT + 2 * i + b
                    split_high(e, w + 1, (W_OUT + b + 1) % 2)
                    for th in range(2):
                        e.wait_ge(sems["dense_done"], BASE + 2 * w + th + 1)
                        e.wait_ge(sems["x_turned"], BASE + 4 * i + 2 * b - 2)
                        e.activation(x_t[:, b, th * HALF:(th + 1) * HALF], bank(4 + th), ACT.Copy).then_inc(sems["dense_evac"], 1)

        def out_pool(e):
            with e.Fori(0, KT // 2) as i:
                for b in range(2):
                    split_low(e, W_OUT + 2 * i + b + 1, (W_OUT + b + 1) % 2)

        def out_dve(e):
            for n in range(NT // 2):
                e.wait_ge(sems[f"x_loaded{n}"], BASE + 32)
            with e.Fori(0, KT // 2) as i:
                for b in range(2):
                    for th in range(2):
                        n = 4 * i + 2 * b + th
                        e.wait_ge(sems["x_turned"], BASE + n + 1)
                        dst = x_sb[:, 4 * th:4 * th + 4, ds((2 * i + b) * P, P)]
                        e.tensor_tensor(dst, dst, heads(bank(2 + th)), ALU.add).then_inc(sems["x1_ready"], 1)

        W_F1 = W_FF + 2

        def ff_loop(e, step):
            step(0, W_FF, W_FF % 2, 0, True, False)
            with e.Fori(0, (NF - 2) // 2) as i:
                for r in range(2):
                    step(2 * i + 1 + r, W_F1 + 6 * i + 3 * r, (W_F1 + 3 * r) % 2, (1 + r) % 2, False, False)
            step(NF - 1, W_F1 + 3 * (NF - 2), (W_F1 + 3 * (NF - 2)) % 2, (NF - 1) % 2, False, False)
            step(NF, W_F1 + 3 * (NF - 1) - 2, (W_F1 + 3 * (NF - 1)) % 2, NF % 2, False, True)

        def ff_sync(e):
            def step(f, w, b, fp, first, last):
                if not last and not first:
                    load_tile(e, w, b, w_gate[:, :, ds(f * P, P)])
                    load_tile(e, w + 1, 1 - b, w_up[:, :, ds(f * P, P)])
                if not first:
                    load_tile(e, w + 2, b, w_down[:, f - 1, :].rearrange("p (k c) -> p k c", c=P))
            ff_loop(e, step)

        def ff_pe(e):
            e.wait_ge(sems["norm_l"], BASE + 2 * NT)

            def product(w, b, th, dst):
                e.wait_ge(sems["wl_ready"], BASE + w + 1)
                cols = slice(th * HALF, (th + 1) * HALF)
                for k in range(KT):
                    e.matmul(dst, w_h[:, b, k], act_h[:, k, cols], start=(k == 0), stop=False)
                    e.matmul(dst, w_h[:, b, k], act_l[:, k, cols], start=False, stop=False)
                    mm = e.matmul(dst, w_l[:, b, k], act_h[:, k, cols], start=False, stop=(k == KT - 1))
                mm.then_inc(sems["gu_done"], 1)

            def step(f, w, b, fp, first, last):
                if not last:
                    for th in range(2):
                        e.wait_ge(sems["ff_silu"], BASE + 2 * f + th - 1)
                        product(w, b, th, bank(th))
                    for th in range(2):
                        e.wait_ge(sems["ff_mul"], BASE + 2 * f + th - 1)
                        product(w + 1, 1 - b, th, bank(2 + th))
                if not first:
                    e.wait_ge(sems["wl_ready"], BASE + w + 3)
                    e.wait_ge(sems["ff_low"], BASE + 2 * f)
                    for c in range(2 * NT):
                        t, n = c // 2, c % 2
                        e.wait_ge(sems["x_added"], BASE + 16 * (f - 1) + c - 3)
                        rows = slice(t * P, (t + 1) * P)
                        dst = bank(4 + c % 4)
                        e.matmul(dst, ff_h[:, 1 - fp, rows], w_h[:, b, 4 * n:4 * n + 4, :], start=True, stop=False)
                        e.matmul(dst, ff_h[:, 1 - fp, rows], w_l[:, b, 4 * n:4 * n + 4, :], start=False, stop=False)
                        e.matmul(dst, ff_l[:, 1 - fp, rows], w_h[:, b, 4 * n:4 * n + 4, :], start=False, stop=True).then_inc(sems["down_done"], 1)
            ff_loop(e, step)

        def ff_act(e):
            def high(w, b, name, count):
                e.wait_ge(sems[f"w_loaded{b}"], BASE + 8 * (w - b) + 16)
                e.wait_ge(sems[name], BASE + count)
                e.activation(w_h[:, b], w_raw[:, b], ACT.Copy).then_inc(sems["wh_ready"], 1)

            def step(f, w, b, fp, first, last):
                if last:
                    return
                if first:
                    high(w + 1, 1 - b, "dense_done", 2 * W_FF)
                else:
                    high(w + 1, 1 - b, "down_done", 16 * (f - 1))
                for th in range(2):
                    e.wait_ge(sems["gu_done"], BASE + 4 * f + th + 1)
                    e.wait_ge(sems["ff_mul"], BASE + 2 * f + th - 1)
                    e.activation(gs[:, th, :], bank(th), ACT.Silu).then_inc(sems["ff_silu"], 1)
                high(w + 2, b, "gu_done", 4 * f + 2)
                for th in range(2):
                    e.wait_ge(sems["ff_mul"], BASE + 2 * f + th + 1)
                    if not first:
                        e.wait_ge(sems["down_done"], BASE + 16 * (f - 1))
                    e.activation(ff_h[:, fp, th * HALF:(th + 1) * HALF], ffv[:, th, :], ACT.Copy).then_inc(sems["ff_high"], 1)
                if not first:
                    high(w + 3, 1 - b, "gu_done", 4 * f + 4)
            ff_loop(e, step)

        def ff_pool(e):
            def step(f, w, b, fp, first, last):
                if last:
                    return
                split_low(e, w + 1, 1 - b)
                split_low(e, w + 2, b)
                for th in range(2):
                    e.wait_ge(sems["ff_high"], BASE + 2 * f + th + 1)
                    cols = slice(th * HALF, (th + 1) * HALF)
                    e.tensor_tensor(ff_l[:, fp, cols], ffv[:, th, :], ff_h[:, fp, cols].bitcast(F32), ALU.subtract).then_inc(sems["ff_low"], 1)
                if not first:
                    split_low(e, w + 3, 1 - b)
            ff_loop(e, step)

        def ff_dve(e):
            def normed(t):
                if t == 0:
                    e.wait_ge(sems["gain_loaded"], BASE + 48)
                e.wait_ge(sems["norm_rstd"], BASE + 2 * NT + t + 1)
                e.scalar_tensor_tensor(out=x_sb[:, t, :], in0=x_sb[:, t, :], scalar=rstd[:, t:t + 1], in1=gain_row[:, :],
                                       op0=ALU.mult, op1=ALU.mult).then_inc(sems["out_ready"], 1)

            def step(f, w, b, fp, first, last):
                if not last:
                    for th in range(2):
                        e.wait_ge(sems["gu_done"], BASE + 4 * f + th + 3)
                        e.wait_ge(sems["ff_silu"], BASE + 2 * f + th + 1)
                        e.wait_ge(sems["ff_low"], BASE + 2 * f + th - 1)
                        e.tensor_tensor(ffv[:, th, :], bank(2 + th), gs[:, th, :], ALU.mult).then_inc(sems["ff_mul"], 1)
                if not first:
                    for c in range(2 * NT):
                        t, n = c // 2, c % 2
                        e.wait_ge(sems["down_done"], BASE + 16 * (f - 1) + c + 1)
                        dst = x_sb[:, t, n * HALF:(n + 1) * HALF]
                        e.tensor_tensor(dst, dst, bank(4 + c % 4), ALU.add).then_inc(sems["x_added"], 1)
                        if last and n == 1 and t >= 2:
                            normed(t - 2)
                if last:
                    for t in range(NT - 2, NT):
                        normed(t)
            ff_loop(e, step)

        def last_act(e):
            for t in range(NT):
                e.wait_ge(sems["x_added"], BASE + 16 * (NF - 1) + 2 * t + 2)
                e.wait_ge(sems["norm_ssq"], BASE + 2 * NT + t)
                e.activation(junk, x_sb[:, t, :], ACT.Square, accum_out=ssq[:, t:t + 1]).then_inc(sems["norm_ssq"], 1)
                e.wait_ge(sems["norm_ssq"], BASE + 2 * NT + t + 1)
                e.activation(lnv[:, t:t + 1], ssq[:, t:t + 1], ACT.Ln, scale=1.0 / D, bias=eps_col[:, 0:1]).then_inc(sems["norm_ln"], 1)
                e.wait_ge(sems["norm_ln"], BASE + 2 * NT + t + 1)
                e.activation(rstd[:, t:t + 1], lnv[:, t:t + 1], ACT.Exp, scale=-0.5).then_inc(sems["norm_rstd"], 1)

        def last_sync(e):
            for t in range(NT):
                e.wait_ge(sems["out_ready"], BASE + t + 1)
                e.dma_start(out_rows[:, t, :], x_sb[:, t, :]).then_inc(sems["out_stored"], 16)
            e.wait_ge(sems["out_stored"], BASE + 16 * NT)

        CONSTS_FIRST = 3
        CONSTS = 12 + 5 + 2 * LEVELS + 3 * LEVELS + 1 + 2

        @block.sync
        def _(e):
            for n in range(NT // 2):
                e.dma_start(x_sb[:, 2 * n:2 * n + 2, :], x_rows[:, 2 * n:2 * n + 2, :]).then_inc(sems[f"x_loaded{n}"], 16)
            e.dma_start(gain_row[:, :], a["norm1"][0].partition_broadcast(P)).then_inc(sems["gain_loaded"], 16)
            e.dma_start(cw_rows[0:4 * NC, :], a["dn_conv"][0].rearrange("k (c p) -> (k c) p", p=P)).then_inc(sems["small_loaded"], 16)
            e.dma_start(dt_row[:, :], a["dn_dt_bias"][0].partition_broadcast(P)).then_inc(sems["rows_loaded"], 16)
            e.dma_start(rate_log[:, :], a["dn_a_log"][0].partition_broadcast(P)).then_inc(sems["rows_loaded"], 16)
            first_sync(e)
            e.wait_ge(sems["norm_xn"], BASE + NT)
            for first, n, width, name in ((0, SBH, SBD, "sb_gain"), (SBW, DNH, P, "dn_gain"), (SBW + DNW, 4, HGD, "hg_gain")):
                for h in range(n):
                    at = first + h * width
                    e.dma_start(gain_row[:, at:at + width], a[name][0].partition_broadcast(P)).then_inc(sems["gains_loaded"], 16)
            lead_sync(e)
            load_tile(e, W_OUT, W_OUT % 2, w_out[:, :, 0:P])
            load_tile(e, W_OUT + 1, (W_OUT + 1) % 2, w_out[:, :, P:2 * P])
            mixed_to_dram(e)
            mixer_sync(e)
            e.wait_ge(sems["act_low"], BASE + 2 * NT)
            e.wait_ge(sems["fin"], BASE + NT)
            e.dma_start(gain_row[:, :], a["norm2"][0].partition_broadcast(P)).then_inc(sems["gain_loaded"], 16)
            for n in range(NT // 2):
                e.dma_start(x_sb[:, 2 * n:2 * n + 2, :], x_rows[:, 2 * n:2 * n + 2, :]).then_inc(sems[f"x_loaded{n}"], 16)
            out_sync(e)
            load_tile(e, W_FF, W_FF % 2, w_gate[:, :, 0:P])
            load_tile(e, W_FF + 1, (W_FF + 1) % 2, w_up[:, :, 0:P])
            e.wait_ge(sems["norm_xn"], BASE + 2 * NT)
            e.dma_start(gain_row[:, :], a["final_norm"].partition_broadcast(P)).then_inc(sems["gain_loaded"], 16)
            ff_sync(e)
            last_sync(e)

        @block.gpsimd
        def _(e):
            assert masks(e) == CONSTS
            first_pool(e)
            mix_pool(e)
            mixer_pool(e)
            out_pool(e)
            ff_pool(e)

        @block.scalar
        def _(e):
            e.preload_act_table_set("natural_log_exp_and_others")
            e.wait_ge(sems["consts"], CONSTS_FIRST)
            norm_act(e, 0)
            first_act(e)
            mix_act(e)
            decay_act(e)
            mixer_act(e)
            out_act(e)
            norm_act(e, 1)
            ff_act(e)
            last_act(e)

        @block.vector
        def _(e):
            norm_dve(e, 0)
            e.wait_ge(sems["consts"], CONSTS)
            first_dve(e)
            mix_dve(e)
            decay_dve(e)
            mixer_dve(e)
            out_dve(e)
            norm_dve(e, 1)
            ff_dve(e)

        @block.tensor
        def _(e):
            e.wait_ge(sems["consts"], CONSTS_FIRST)
            norm_pe(e, 0)
            e.wait_ge(sems["consts"], CONSTS)
            e.wait_ge(sems["norm_l"], BASE + NT)
            first_pe(e)
            mix_pe(e)
            decay_pe(e)
            mixer_pe(e)
            out_pe(e)
            norm_pe(e, 1)
            ff_pe(e)


INPUTS = ("x", "norm1", "w_in", "sb_gain", "dn_conv", "dn_a_log", "dn_dt_bias", "dn_gain", "hg_lb_logits", "hg_gain",
          "w_out", "norm2", "w_gate", "w_up", "w_down", "final_norm")


def kernel(**inputs):
    import numpy as np
    import concourse.bacc as bacc
    from concourse.bass_utils import run_bass_kernel_spmd

    nc = bacc.Bacc("TRN2", target_bir_lowering=False, num_devices=1)
    arrays, args = {}, {}
    for name in INPUTS:
        arrays[f"in_{name}"] = np.ascontiguousarray(inputs[name])
        args[name] = nc.dram_tensor(f"in_{name}", arrays[f"in_{name}"].shape, F32, kind="ExternalInput").ap()
    out = nc.dram_tensor("out", inputs["x"].shape, F32, kind="ExternalOutput").ap()
    trunk_program(nc, args, out)
    got = run_bass_kernel_spmd(nc, [arrays], core_ids=[0])
    return got.results[0]["out"]
```
